# Optimizing a Trainium2 kernel written in Bass

```python
import math
import jax, jax.numpy as jnp
from jax import lax
import numpy as np

D_MODEL = 1024
BATCH = 1
SEQ = 512
DEPTH = 2

N_A_LAYERS = DEPTH // 2
N_B_LAYERS = DEPTH - N_A_LAYERS
CONV_WIDTH = 3
FFN_HIDDEN = -(-8 * D_MODEL // (3 * 256)) * 256
N_HEADS = 16
N_KV_GROUPS = 4
HEADS_PER_GROUP = N_HEADS // N_KV_GROUPS
HEAD_DIM = 64
L_CMP = 32
D_CMP = 16
L_SLC = 64
N_SEL = 16
WINDOW = 512
CMP_HIDDEN = 256
Q_BLOCK = 64
N_KV_SETS = 6
RMS_EPS = 1e-5
NEG_INF = -1e30
FORCE_BONUS = 1e4


def rms_norm(x, g):
    xf = x.astype(jnp.float32)
    y = xf * lax.rsqrt(jnp.mean(xf * xf, axis=-1, keepdims=True) + RMS_EPS)
    return (y * g.astype(jnp.float32)).astype(x.dtype)

def short_conv_mixer(h, w_in, conv_w, w_out):
    b_gate, c_gate, v = jnp.split(h @ w_in, 3, axis=-1)
    u = lax.conv_general_dilated(
        c_gate * v, conv_w[:, None, :], window_strides=(1,),
        padding=((CONV_WIDTH - 1, 0),), dimension_numbers=("NWC", "WIO", "NWC"),
        feature_group_count=D_MODEL)
    return (b_gate * u) @ w_out

def swiglu(h, w_gu, w_down):
    g, u = jnp.split(h @ w_gu, 2, axis=-1)
    return (jax.nn.silu(g) * u) @ w_down

def compress(kv_raw, pe, w1, w2):
    bsz, seq = kv_raw.shape[0], kv_raw.shape[1]
    n_cmp = (seq - L_CMP) // D_CMP + 1
    idx = jnp.arange(n_cmp)[:, None] * D_CMP + jnp.arange(L_CMP)[None, :]
    blocks = kv_raw[:, idx] + pe[None, None, :, None, :]
    blocks = blocks.transpose(0, 1, 3, 2, 4).reshape(bsz, n_cmp, N_KV_GROUPS, L_CMP * HEAD_DIM)
    return jax.nn.silu(blocks @ w1) @ w2

def shared_kv(h, kv_norm, w_kv, pe_k, w1_k, w2_k, pe_v, w1_v, w2_v):
    bsz, seq, _ = h.shape
    kv = (rms_norm(h, kv_norm) @ w_kv).reshape(bsz, seq, N_KV_SETS, N_KV_GROUPS, HEAD_DIM)
    k_cmp = compress(kv[:, :, 0], pe_k, w1_k, w2_k)
    v_cmp = compress(kv[:, :, 1], pe_v, w1_v, w2_v)
    return (k_cmp, v_cmp, kv[:, :, 2], kv[:, :, 3], kv[:, :, 4], kv[:, :, 5])

def nsa_mixer(h, w_qg, w_o, k_cmp, v_cmp, k_slc, v_slc, k_win, v_win):
    bsz, seq, _ = h.shape
    G, HPG, dh = N_KV_GROUPS, HEADS_PER_GROUP, HEAD_DIM
    qg = h @ w_qg
    q = (qg[..., :N_HEADS * dh] * (dh ** -0.5)).reshape(bsz, seq, G, HPG, dh)
    gates = jax.nn.sigmoid(qg[..., N_HEADS * dh:].astype(jnp.float32)).reshape(bsz, seq, G, HPG, 3)

    slopes = jnp.exp2(-8.0 * jnp.arange(1, N_HEADS + 1, dtype=jnp.float32) / N_HEADS).reshape(G, HPG)

    n_cmp = k_cmp.shape[1]
    cmp_start = jnp.arange(n_cmp) * D_CMP
    cmp_end = cmp_start + L_CMP - 1
    cmp_center = cmp_end.astype(jnp.float32) - (L_CMP - 1) / 2.0
    n_slc = seq // L_SLC
    n_sel = min(N_SEL, n_slc)
    slc_start = jnp.arange(n_slc) * L_SLC
    overlap = ((cmp_start[:, None] < slc_start[None, :] + L_SLC)
               & (cmp_start[:, None] + L_CMP > slc_start[None, :])).astype(jnp.float32)

    k_blk = k_slc.reshape(bsz, n_slc, L_SLC, G, dh).transpose(0, 3, 1, 2, 4)
    v_blk = v_slc.reshape(bsz, n_slc, L_SLC, G, dh).transpose(0, 3, 1, 2, 4)
    pad = ((0, 0), (WINDOW, 0), (0, 0), (0, 0))
    k_win_pad = jnp.pad(k_win, pad)
    v_win_pad = jnp.pad(v_win, pad)
    b_ix = jnp.arange(bsz)[:, None, None, None]
    g_ix = jnp.arange(G)[None, :, None, None]
    j_blk = jnp.arange(n_slc)

    def one_block(qb):
        q0 = qb * Q_BLOCK
        t = q0 + jnp.arange(Q_BLOCK)
        tf = t.astype(jnp.float32)
        qblk = lax.dynamic_slice_in_dim(q, q0, Q_BLOCK, axis=1)
        gblk = lax.dynamic_slice_in_dim(gates, q0, Q_BLOCK, axis=1)

        s = jnp.einsum("bqghd,bngd->bghqn", qblk, k_cmp).astype(jnp.float32)
        vis = cmp_end[None, :] <= t[:, None]
        s = s - slopes[:, :, None, None] * (tf[:, None] - cmp_center[None, :])
        p_cmp = jax.nn.softmax(jnp.where(vis, s, NEG_INF), axis=-1) * vis
        o_cmp = jnp.einsum("bghqn,bngd->bqghd", p_cmp.astype(v_cmp.dtype), v_cmp)

        imp = jnp.einsum("bghqn,nj->bgqj", p_cmp, overlap)
        cur = t // L_SLC
        valid = j_blk[None, :] <= cur[:, None]
        forced = ((j_blk[None, :] == 0) | (j_blk[None, :] == cur[:, None])
                  | (j_blk[None, :] == cur[:, None] - 1))
        imp = jnp.where(valid, imp + FORCE_BONUS * forced, NEG_INF)
        _, sel = lax.top_k(imp, n_sel)
        k_sel = k_blk[b_ix, g_ix, sel]
        v_sel = v_blk[b_ix, g_ix, sel]
        s = jnp.einsum("bqghd,bgqnld->bghqnl", qblk, k_sel).astype(jnp.float32)
        dist = t[None, None, :, None, None] - (sel[..., None] * L_SLC + jnp.arange(L_SLC))
        dist = dist[:, :, None]
        s = s - slopes[:, :, None, None, None] * dist.astype(jnp.float32)
        s = jnp.where(dist >= 0, s, NEG_INF)
        p = jax.nn.softmax(s.reshape(s.shape[:4] + (n_sel * L_SLC,)), axis=-1).reshape(s.shape)
        o_slc = jnp.einsum("bghqnl,bgqnld->bqghd", p.astype(v_sel.dtype), v_sel)

        kw = lax.dynamic_slice_in_dim(k_win_pad, q0, WINDOW + Q_BLOCK, axis=1)
        vw = lax.dynamic_slice_in_dim(v_win_pad, q0, WINDOW + Q_BLOCK, axis=1)
        spos = q0 - WINDOW + jnp.arange(WINDOW + Q_BLOCK)
        d = t[:, None] - spos[None, :]
        m = (d >= 0) & (d < WINDOW) & (spos >= 0)[None, :]
        s = jnp.einsum("bqghd,bkgd->bghqk", qblk, kw).astype(jnp.float32)
        s = s - slopes[:, :, None, None] * d.astype(jnp.float32)
        p = jax.nn.softmax(jnp.where(m, s, NEG_INF), axis=-1)
        o_win = jnp.einsum("bghqk,bkgd->bqghd", p.astype(vw.dtype), vw)

        o = (gblk[..., 0:1] * o_cmp + gblk[..., 1:2] * o_slc + gblk[..., 2:3] * o_win)
        return o.reshape(bsz, Q_BLOCK, N_HEADS * dh).astype(h.dtype)

    out = lax.map(one_block, jnp.arange(seq // Q_BLOCK))
    out = out.transpose(1, 0, 2, 3).reshape(bsz, seq, N_HEADS * dh)
    return out @ w_o

def first_inputs(seed: int = 0) -> dict:
    key = jax.random.key(seed)
    ks = jax.random.split(key, 24)

    def w(k, shape, fan_in):
        return jax.random.normal(k, shape, jnp.float32) * (fan_in ** -0.5)

    def gain(k, shape):
        return 1.0 + 0.02 * jax.random.normal(k, shape, jnp.float32)

    D, F = D_MODEL, FFN_HIDDEN
    kv_w = N_KV_GROUPS * HEAD_DIM
    qg_w = N_HEADS * HEAD_DIM + 3 * N_HEADS
    return {
        "x": jax.random.normal(ks[0], (BATCH, SEQ, D), jnp.float32),
        "a_norm": gain(ks[1], (N_A_LAYERS, D)),
        "a_w_in": w(ks[2], (N_A_LAYERS, D, 3 * D), D),
        "a_conv": w(ks[3], (N_A_LAYERS, CONV_WIDTH, D), CONV_WIDTH),
        "a_w_out": w(ks[4], (N_A_LAYERS, D, D), D),
        "kv_norm": gain(ks[5], (D,)),
        "w_kv": w(ks[6], (D, N_KV_SETS * kv_w), D),
        "cmp_pe_k": 0.02 * jax.random.normal(ks[7], (L_CMP, HEAD_DIM), jnp.float32),
        "cmp_w1_k": w(ks[8], (L_CMP * HEAD_DIM, CMP_HIDDEN), L_CMP * HEAD_DIM),
        "cmp_w2_k": w(ks[9], (CMP_HIDDEN, HEAD_DIM), CMP_HIDDEN),
        "cmp_pe_v": 0.02 * jax.random.normal(ks[10], (L_CMP, HEAD_DIM), jnp.float32),
        "cmp_w1_v": w(ks[11], (L_CMP * HEAD_DIM, CMP_HIDDEN), L_CMP * HEAD_DIM),
        "cmp_w2_v": w(ks[12], (CMP_HIDDEN, HEAD_DIM), CMP_HIDDEN),
        "b_norm": gain(ks[13], (N_B_LAYERS, D)),
        "b_w_qg": w(ks[14], (N_B_LAYERS, D, qg_w), D),
        "b_w_o": w(ks[15], (N_B_LAYERS, N_HEADS * HEAD_DIM, D), N_HEADS * HEAD_DIM),
        "f_norm": gain(ks[16], (DEPTH, D)),
        "f_w_gu": w(ks[17], (DEPTH, D, 2 * F), D),
        "f_w_down": w(ks[18], (DEPTH, F, D), F),
        "final_norm": gain(ks[19], (D,)),
    }

def first_block(x, a_norm, a_w_in, a_conv, a_w_out, kv_norm, w_kv, cmp_pe_k, cmp_w1_k, cmp_w2_k,
              cmp_pe_v, cmp_w1_v, cmp_w2_v, b_norm, b_w_qg, b_w_o, f_norm, f_w_gu, f_w_down,
              final_norm):
    h = x
    shared = None
    for layer in range(DEPTH):
        if layer < N_A_LAYERS:
            i = layer
            h = h + short_conv_mixer(rms_norm(h, a_norm[i]), a_w_in[i], a_conv[i], a_w_out[i])
        else:
            i = layer - N_A_LAYERS
            if shared is None:
                shared = shared_kv(h, kv_norm, w_kv, cmp_pe_k, cmp_w1_k, cmp_w2_k,
                                   cmp_pe_v, cmp_w1_v, cmp_w2_v)
            k_cmp, v_cmp, k_slc, v_slc, k_win, v_win = shared
            h = h + nsa_mixer(rms_norm(h, b_norm[i]), b_w_qg[i], b_w_o[i],
                              k_cmp, v_cmp, k_slc, v_slc, k_win, v_win)
        h = h + swiglu(rms_norm(h, f_norm[layer]), f_w_gu[layer], f_w_down[layer])
    return rms_norm(h, final_norm)


DEPTH_2 = 1

EXPAND = 2
D_MIX = EXPAND * D_MODEL
D_SSD = D_MIX // 2
D_SB = D_MIX - D_SSD
N_SSD_HEADS = D_SSD // HEAD_DIM
N_SB_HEADS = D_SB // HEAD_DIM
SSD_GROUPS = 2
SSD_STATE = 128
CONV_WIDTH_2 = 4
D_CONV = D_SSD + 2 * SSD_GROUPS * SSD_STATE
SSD_CHUNK = 128
SB_BLOCK = 128
D_FF = -(-8 * D_MODEL // (3 * 256)) * 256
N_MOD = 6
EPS = 1e-6
IN_SPLITS = [int(s) for s in np.cumsum([D_SSD, D_CONV, N_SSD_HEADS, D_SB, D_SB])]
D_IN_PROJ = IN_SPLITS[-1] + D_SB


def rms_norm_2(x, w):
    xf = x.astype(jnp.float32)
    y = xf * lax.rsqrt(jnp.mean(xf * xf, axis=-1, keepdims=True) + EPS)
    return (y * w.astype(jnp.float32)).astype(x.dtype)

def causal_depthwise_conv(u, w, b):
    out = lax.conv_general_dilated(
        u, w[:, None, :], window_strides=(1,), padding=[(CONV_WIDTH_2 - 1, 0)],
        dimension_numbers=("NWC", "WIO", "NWC"), feature_group_count=u.shape[-1])
    return out + b

def ssd_chunked(x, dt, a, b_mat, c_mat):
    bsz, seq, n_heads, p = x.shape
    g, n = b_mat.shape[2], b_mat.shape[3]
    e = n_heads // g
    nc, t = seq // SSD_CHUNK, SSD_CHUNK
    xg = (x * dt[..., None]).reshape(bsz, nc, t, g, e, p)
    a_dt = jnp.moveaxis((a * dt).reshape(bsz, nc, t, g, e), 2, -1)
    a_cs = jnp.cumsum(a_dt, axis=-1)
    bm = b_mat.reshape(bsz, nc, t, g, n)
    cm = c_mat.reshape(bsz, nc, t, g, n)
    idx = jnp.arange(t)
    causal = idx[:, None] >= idx[None, :]
    seg = a_cs[..., :, None] - a_cs[..., None, :]
    decay = jnp.exp(jnp.where(causal, seg, -jnp.inf))
    scores = jnp.einsum("bclgn,bcsgn->bcgls", cm, bm)
    y_diag = jnp.einsum("bcgls,bcgels,bcsgep->bclgep", scores, decay, xg)
    decay_states = jnp.exp(a_cs[..., -1:] - a_cs)
    states = jnp.einsum("bclgn,bcgel,bclgep->bcgepn", bm, decay_states, xg)
    chunk_decay = jnp.exp(a_cs[..., -1])

    def step(carry, inp):
        st, dec = inp
        return carry * dec[..., None, None] + st, carry

    init = jnp.zeros_like(states[:, 0])
    _, prev_states = lax.scan(step, init, (jnp.moveaxis(states, 1, 0), jnp.moveaxis(chunk_decay, 1, 0)))
    prev_states = jnp.moveaxis(prev_states, 0, 1)
    y_off = jnp.einsum("bclgn,bcgepn,bcgel->bclgep", cm, prev_states, jnp.exp(a_cs))
    return (y_diag + y_off).reshape(bsz, seq, n_heads, p)

def ssd_mixer(z, xbc, dt_raw, conv_w, conv_b, dt_bias, a_log, d_skip, norm_w):
    bsz, seq, _ = z.shape
    f32 = jnp.float32
    xbc = jax.nn.silu(causal_depthwise_conv(xbc, conv_w, conv_b)).astype(f32)
    xs = xbc[..., :D_SSD]
    bm = xbc[..., D_SSD:D_SSD + SSD_GROUPS * SSD_STATE].reshape(bsz, seq, SSD_GROUPS, SSD_STATE)
    cm = xbc[..., D_SSD + SSD_GROUPS * SSD_STATE:].reshape(bsz, seq, SSD_GROUPS, SSD_STATE)
    xh = xs.reshape(bsz, seq, N_SSD_HEADS, HEAD_DIM)
    dt = jax.nn.softplus(dt_raw.astype(f32) + dt_bias.astype(f32))
    a = -jnp.exp(a_log.astype(f32))
    y = ssd_chunked(xh, dt, a, bm, cm) + d_skip.astype(f32)[:, None] * xh
    y = y.reshape(bsz, seq, D_SSD) * jax.nn.silu(z.astype(f32))
    yg = y.reshape(bsz, seq, SSD_GROUPS, D_SSD // SSD_GROUPS)
    yg = yg * lax.rsqrt(jnp.mean(yg * yg, axis=-1, keepdims=True) + EPS)
    return (yg.reshape(bsz, seq, D_SSD) * norm_w.astype(f32)).astype(z.dtype)

def stick_breaking_mixer(q, k, v, q_norm_w, k_norm_w):
    bsz, seq, _ = q.shape
    f32 = jnp.float32
    q = rms_norm_2(q.reshape(bsz, seq, N_SB_HEADS, HEAD_DIM), q_norm_w).astype(f32).transpose(0, 2, 1, 3)
    k = rms_norm_2(k.reshape(bsz, seq, N_SB_HEADS, HEAD_DIM), k_norm_w).astype(f32).transpose(0, 2, 1, 3)
    vh = v.reshape(bsz, seq, N_SB_HEADS, HEAD_DIM).astype(f32).transpose(0, 2, 1, 3)
    scale = HEAD_DIM ** -0.5
    outs = []
    for blk in range(seq // SB_BLOCK):
        start, end = blk * SB_BLOCK, (blk + 1) * SB_BLOCK
        qb, kp, vp = q[:, :, start:end], k[:, :, :end], vh[:, :, :end]
        logits = jnp.einsum("bhqd,bhkd->bhqk", qb, kp) * scale
        t_pos = start + jnp.arange(SB_BLOCK)
        s_pos = jnp.arange(end)
        strict = s_pos[None, :] < t_pos[:, None]
        log_rem = jnp.where(strict, jax.nn.log_sigmoid(-logits), 0.0)
        log_between = lax.cumsum(log_rem, axis=3, reverse=True) - log_rem
        weights = jnp.where(strict, jnp.exp(jax.nn.log_sigmoid(logits) + log_between), 0.0)
        outs.append(jnp.einsum("bhqk,bhkd->bhqd", weights, vp))
    o = jnp.concatenate(outs, axis=2)
    return o.transpose(0, 2, 1, 3).reshape(bsz, seq, D_SB).astype(v.dtype)

def second_inputs(seed: int = 0) -> dict:
    key = jax.random.key(seed)
    ks = jax.random.split(key, 24)
    f32 = jnp.float32
    nrm = lambda k, shape, s: jax.random.normal(k, shape, f32) * s
    dt0 = jnp.exp(jax.random.uniform(ks[8], (DEPTH_2, N_SSD_HEADS), f32,
                                     float(np.log(1e-3)), float(np.log(1e-1))))
    dt_bias = dt0 + jnp.log(-jnp.expm1(-dt0))
    return {
        "x": nrm(ks[0], (BATCH, SEQ, D_MODEL), 1.0),
        "c": nrm(ks[1], (BATCH, D_MODEL), 1.0),
        "w_ada": nrm(ks[2], (DEPTH_2, D_MODEL, N_MOD * D_MODEL), 0.5 * D_MODEL ** -0.5),
        "b_ada": nrm(ks[3], (DEPTH_2, N_MOD * D_MODEL), 0.01),
        "norm1_w": 1.0 + nrm(ks[4], (DEPTH_2, D_MODEL), 0.02),
        "w_in": nrm(ks[5], (DEPTH_2, D_MODEL, D_IN_PROJ), D_MODEL ** -0.5),
        "conv_w": nrm(ks[6], (DEPTH_2, CONV_WIDTH_2, D_CONV), CONV_WIDTH_2 ** -0.5),
        "conv_b": nrm(ks[7], (DEPTH_2, D_CONV), 0.01),
        "dt_bias": dt_bias,
        "a_log": jnp.log(jax.random.uniform(ks[9], (DEPTH_2, N_SSD_HEADS), f32, 1.0, 16.0)),
        "d_skip": 1.0 + nrm(ks[10], (DEPTH_2, N_SSD_HEADS), 0.02),
        "ssd_norm_w": 1.0 + nrm(ks[11], (DEPTH_2, D_SSD), 0.02),
        "q_norm_w": 1.0 + nrm(ks[12], (DEPTH_2, HEAD_DIM), 0.02),
        "k_norm_w": 1.0 + nrm(ks[13], (DEPTH_2, HEAD_DIM), 0.02),
        "w_out": nrm(ks[14], (DEPTH_2, D_MIX, D_MODEL), D_MIX ** -0.5),
        "norm2_w": 1.0 + nrm(ks[15], (DEPTH_2, D_MODEL), 0.02),
        "w_gate": nrm(ks[16], (DEPTH_2, D_MODEL, D_FF), D_MODEL ** -0.5),
        "w_up": nrm(ks[17], (DEPTH_2, D_MODEL, D_FF), D_MODEL ** -0.5),
        "w_down": nrm(ks[18], (DEPTH_2, D_FF, D_MODEL), D_FF ** -0.5),
    }

def second_block(x, c, w_ada, b_ada, norm1_w, w_in, conv_w, conv_b, dt_bias, a_log, d_skip,
              ssd_norm_w, q_norm_w, k_norm_w, w_out, norm2_w, w_gate, w_up, w_down):
    cond = jax.nn.silu(c)
    for layer in range(DEPTH_2):
        mod = (cond @ w_ada[layer] + b_ada[layer])[:, None, :]
        sh1, sc1, g1, sh2, sc2, g2 = jnp.split(mod, N_MOD, axis=-1)
        h = rms_norm_2(x, norm1_w[layer]) * (1.0 + sc1) + sh1
        proj = h @ w_in[layer]
        z, xbc, dt_raw, q, k, v = jnp.split(proj, IN_SPLITS, axis=-1)
        y_ssd = ssd_mixer(z, xbc, dt_raw, conv_w[layer], conv_b[layer], dt_bias[layer],
                          a_log[layer], d_skip[layer], ssd_norm_w[layer])
        y_sb = stick_breaking_mixer(q, k, v, q_norm_w[layer], k_norm_w[layer])
        mix = jnp.concatenate([y_ssd, y_sb], axis=-1) @ w_out[layer]
        x = x + g1 * mix
        h = rms_norm_2(x, norm2_w[layer]) * (1.0 + sc2) + sh2
        ffn = (jax.nn.silu(h @ w_gate[layer]) * (h @ w_up[layer])) @ w_down[layer]
        x = x + g2 * ffn
    return x


def setup_inputs(seed=0):
    out = dict(first_inputs(seed))
    for name, value in second_inputs(seed + 1).items():
        if name != "x":
            out[name + "_2"] = value
    return out


def reference(
    x, a_norm, a_w_in, a_conv, a_w_out, kv_norm, w_kv, cmp_pe_k, cmp_w1_k, cmp_w2_k, cmp_pe_v,
    cmp_w1_v, cmp_w2_v, b_norm, b_w_qg, b_w_o, f_norm, f_w_gu, f_w_down, final_norm, c_2,
    w_ada_2, b_ada_2, norm1_w_2, w_in_2, conv_w_2, conv_b_2, dt_bias_2, a_log_2, d_skip_2,
    ssd_norm_w_2, q_norm_w_2, k_norm_w_2, w_out_2, norm2_w_2, w_gate_2, w_up_2, w_down_2,
):
    x = first_block(
        x, a_norm, a_w_in, a_conv, a_w_out, kv_norm, w_kv, cmp_pe_k, cmp_w1_k, cmp_w2_k,
        cmp_pe_v, cmp_w1_v, cmp_w2_v, b_norm, b_w_qg, b_w_o, f_norm, f_w_gu, f_w_down,
        final_norm,
    )
    return second_block(
        x, c_2, w_ada_2, b_ada_2, norm1_w_2, w_in_2, conv_w_2, conv_b_2, dt_bias_2, a_log_2,
        d_skip_2, ssd_norm_w_2, q_norm_w_2, k_norm_w_2, w_out_2, norm2_w_2, w_gate_2, w_up_2,
        w_down_2,
    )


_drawn_inputs = setup_inputs


def setup_inputs(seed=0):
    import zlib

    import numpy as np

    out = dict(_drawn_inputs(seed))
    spreads = {}
    factors = {'kv_norm': 8.0,
     'cmp_pe_k': 8.0,
     'cmp_pe_v': 8.0,
     'b_norm': 8.0,
     'f_norm': 3.443,
     'final_norm': 2.725,
     'b_ada_2': 4.266,
     'norm1_w_2': 8.0,
     'conv_b_2': 64.0,
     'd_skip_2': 200.0,
     'ssd_norm_w_2': 32.627,
     'q_norm_w_2': 8.0,
     'k_norm_w_2': 21.839,
     'norm2_w_2': 8.0}
    for name, (base, spread) in spreads.items():
        noise = np.random.default_rng([zlib.crc32(name.encode()), seed]).standard_normal(out[name].shape)
        drawn = base * np.exp(spread * noise) if base else spread * noise
        out[name] = __import__('jax').numpy.asarray(drawn.astype(out[name].dtype))
    for name, factor in factors.items():
        out[name] = (out[name] * factor).astype(out[name].dtype)
    return out
```

```python
from contextlib import ExitStack

import concourse.bass as bass
from concourse import mybir

F32 = mybir.dt.float32
F32R = mybir.dt.float32r
ALU = mybir.AluOpType
ACT = mybir.ActivationFunctionType
AX_X = mybir.AxisListType.X

P = 128
T = 512
D = 1024
DC = D // P
F = 2816
FC = F // P
F1, F2 = 12, 10
NB = 4
KMAX = 2048
QB = T // P
HD = 64
NH = 16
NCMP = 31
CG = 32
BIG = 3.0e30
EPS1 = 1e-5
EPS2 = 1e-6
DS = bass.ds

SEGMENTS = [
    ("win", "A", 12), ("wout", "A", 4),
    ("gu0a", "A", F1), ("dn0a", "B", 8), ("gu0b", "A", F2), ("dn0b", "C", 8),
    ("wkv", "A", 6), ("wq", "A", 4), ("wo", "A", 4),
    ("gu1a", "A", F1), ("dn1a", "B", 8), ("gu1b", "A", F2), ("dn1b", "C", 8),
    ("qkv", "A", 12), ("xbc", "A", 6), ("zg", "A", 4), ("wout2", "D", 8),
    ("gu2a", "A", F1), ("dn2a", "B", 8), ("gu2b", "A", F2), ("dn2b", "C", 8),
]
KINDS = {"A": (DC, 2), "B": (F1, 1), "C": (F2, 1), "D": (2 * DC, 1)}


class Segment:

    def __init__(self, name, kind, units, unit0, tile0, at0):
        self.name, self.kind, self.units = name, kind, units
        self.chunks, self.tiles = KINDS[kind]
        self.size = self.chunks * self.tiles * P
        self.unit0, self.tile0, self.at0 = unit0, tile0, at0
        self.upb = NB // self.tiles
        self.bodies = units // self.upb


def plan():
    segs, unit, tile, at = {}, 0, 0, {k: 0 for k in KINDS}
    size, after = [], []
    for name, kind, units in SEGMENTS:
        s = segs[name] = Segment(name, kind, units, unit, tile, at[kind])
        assert s.bodies * s.upb == units
        for u in range(units):
            size.append(s.size)
            after.append(tile + s.tiles * (u + 1))
        unit, tile, at[kind] = unit + units, tile + s.tiles * units, at[kind] + units
    return segs, size, after


SEGS, UNIT_SIZE, TILES_AFTER = plan()
UNITS = len(UNIT_SIZE)

PARAMS = [("a_norm", 8), ("f_norm0", 8), ("kv_norm", 8), ("b_norm", 8), ("f_norm1", 8), ("final", 8),
          ("norm1", 8), ("norm2", 8), ("conv1", 24), ("conv2", 48), ("conv2b", 12), ("ssdn", 8),
          ("dskip", 8), ("qn", 1), ("kn", 1), ("bada", 48), ("cond", 8), ("pek", 16), ("pev", 16),
          ("dtb", 16), ("alog", 16), ("gatew", 384), ("dtw", 128), ("w2k", 256), ("w2v", 128)]
COL, _n = {}, 0
for _name, _w in PARAMS:
    COL[_name] = _n
    _n += _w
NPAR = _n


C_IDENT, C_BONES, C_SLOPES, C_VIS = 0, P, 2 * P, 2 * P + NH
C_DIST = C_VIS + 1
C_DISTC = C_DIST + T
C_TRI = C_DISTC + QB * CG
C_MASK = C_TRI + P
C_MASKL = C_MASK + P
C_END = C_MASKL + P


class Tally:

    def __init__(self, eng, sem):
        self.eng, self.sem, self.n, self.var = eng, sem, 0, 0

    def mark(self, ins, by=1):
        ins.then_inc(self.sem, by)
        self.n += by

    def wait(self):
        self.eng.wait_ge(self.sem, self.var + self.n if not isinstance(self.var, int) else self.n)


def loop(eng, first, last, tallies, body):
    if last - first == 1:
        body(first)
        return
    if last <= first:
        return
    with eng.Fori(first, last) as i:
        start = [t.n for t, _ in tallies]
        outer = [t.var for t, _ in tallies]
        for t, k in tallies:
            t.var = t.var + (i - first) * k
        body(i)
        for (t, k), n, var in zip(tallies, start, outer):
            assert t.n - n == k, (t.n - n, k)
            t.var = var
            t.n = n + k * (last - first)


def two_blocks(nc, x_in, wA, wB, wC, wD, wada, w1k, w1v, par_in, consts, out):
    streams = {"A": wA, "B": wB, "C": wC, "D": wD}
    ctx = ExitStack()
    with ctx:
        arena0 = (nc.sbuf_base + 31) // 32 * 32
        KB = 1024
        ctx.enter_context(nc.sbuf_tensor("arena", [P, 207 * KB + 512], mybir.dt.uint8))

        def at(name, kb, shape, dt=F32):
            size = 4
            for n in shape[1:]:
                size *= n
            assert kb * KB + size <= 207.5 * KB, name
            return nc.alloc_sbuf_tensor_at(name, shape, dt, offset=arena0 + int(kb * KB))

        def sem(name):
            return ctx.enter_context(nc.semaphore(name))

        X = at("X", 0, [P, DC, T])
        Hh = at("Hh", 16, [P, DC, T], F32R)
        Hl = at("Hl", 32, [P, DC, T], F32R)
        Gh = at("Gh", 48, [P, F1, T], F32R)
        Gl = at("Gl", 72, [P, F1, T], F32R)
        WR = at("WR", 96, [P, 2, KMAX])
        WH = at("WH", 112, [P, 2, KMAX], F32R)
        WL = at("WL", 128, [P, 2, KMAX], F32R)
        SQ = at("SQ", 144, [P, 2, T])
        RT = at("RT", 148, [P, T])
        RS = at("RS", 150, [P, T])
        XN = at("XN", 152, [P, 2, T])
        par = at("par", 200, [P, NPAR])
        ones = at("ones", 205, [P, P])
        EPSC = at("EPSC", 205.75, [P, 2])
        CSIL = at("CSIL", 205.8125, [P, DC])
        MOD = at("MOD", 205.5, [P, 48])
        CT = at("CT", 156, [P, 2, T])
        CV = at("CV", 160, [P, T + 8])
        CU = at("CU", 163, [P, T])
        HT = at("HT", 196, [P, T])
        SG = at("SG", 160, [P, 2, T])
        HF = at("HF", 164, [P, T])
        AW = at("AW", 166, [P, 2, KMAX])
        AACC = at("AACC", 182, [P, 24 * P])

        KV = at("KV", 48, [P, 12, T])
        QT = at("QT", 72, [P, DC, T])
        VT = at("VT", 88, [P, 2, QB, 256])
        OC = at("OC", 144, [P, DC, T])
        W1 = [at("W1K", 160, [P, 16, 256]), at("W1V", 176, [P, 16, 256])]
        RW = at("RW", 192, [P, 4, T])
        XJ = at("XJ", 60, [P, 2, 4, CG])
        HID = at("HID", 61, [P, 2, 4, CG])
        HIDR = at("HIDR", 192, [P, 2, 4, 4, CG])
        KC = at("KC", 62, [P, 4 * CG])
        VC = at("VC", 63, [P, 4, HD])
        GT = at("GT", 68, [P, QB, 3 * NH])
        GWH = at("GWH", 69, [P, DC, 3 * NH], F32R)
        GWL = at("GWL", 70.5, [P, DC, 3 * NH], F32R)
        DIST = at("DIST", 48, [P, T])
        XO = at("XO", 50, [P, T])
        NMX = at("NMX", 52, [P, 2, 32])
        SMX = at("SMX", 52.5, [P, 2, 32])
        DISTC = at("DISTC", 53, [P, QB, CG])
        CMX = at("CMX", 53.5, [P, 3, NH])
        SC = at("SC", 176, [P, T])
        CB = at("CB", 178, [P, T])
        SE = at("SE", 180, [P, T])
        PCT = at("PCT", 192, [P, 4, T])
        PT = at("PT", 160, [P, 2, QB, T])
        PB = at("PB", 176, [P, 4, T])
        VS = at("VS", 184, [P, 2, QB, P])
        BIAS = at("BIAS", 188, [P, 4, T])
        QS = at("QS", 196, [P, 2, T])
        QKV = at("QKV", 144, [P, 12, T])
        VTS = at("VTS", 168, [P, QB, T])
        SQ2 = at("SQ2", 176, [P, 2, T])
        RT2 = at("RT2", 180, [P, 2, T])
        XM = at("XM", 176, [P, 4, T])
        EE = at("EE", 184, [P, 4, T])
        CC = at("CC", 192, [P, 4, T])
        PTS = [at("PTSa", 64, [P, QB, T]), at("PTSb", 88, [P, QB, T])]
        XB = at("XB", 144, [P, 12, T])
        RB = at("RB", 168, [P, T + 8])
        CA = at("CA", 171, [P, 2, T])
        CH = at("CH", 168, [P, 12, P])
        XDT = at("XDT", 174, [P, NH, HD])
        XDD = at("XDD", 178, [P, NH, HD])
        LM = at("LM", 182, [P, NH, P])
        YC = at("YC", 190, [P, NH, HD])
        PREV = at("PREV", 194, [P, NH, HD])
        BTK = at("BTK", 198, [P, 2, P])
        SCR = at("SCR", 199, [P, 2, P])
        DT = at("DT", 64, [P, QB, NH])
        DTE = at("DTE", 64.25, [P, QB, NH])
        ADT = at("ADT", 64.5, [P, QB, NH])
        CS = at("CS", 64.75, [P, QB, NH])
        NCS = at("NCS", 65, [P, QB, NH])
        EX = at("EX", 65.25, [P, 3, NH])
        CSL = at("CSL", 65.5, [P, NH])
        AN = at("AN", 65.625, [P, NH])
        ADTC = at("ADTC", 65.75, [P, NH])
        DWH = at("DWH", 66, [P, DC, NH], F32R)
        DWL = at("DWL", 66.5, [P, DC, NH], F32R)
        SZ = at("SZ", 168, [P, 2, T])
        SQ3 = at("SQ3", 172, [P, 2, T])
        RZ = at("RZ", 176, [P, 2, T])
        XN2 = at("XN2", 180, [P, 2, T])
        GM = at("GM", 205.6875, [P, DC])
        ident = at("ident", 206, [P, P])
        bones = at("bones", 206.5, [P, P])
        slopes = at("slopes", 207, [P, NH + 1])
        visrow = slopes[:, NH:NH + 1]

        gw = COL["gatew"]
        TRI, MASK, MASKL = par[:, gw:gw + P], par[:, gw + P:gw + 2 * P], par[:, gw + 2 * P:gw + 3 * P]
        PS = ctx.enter_context(nc.psum_tensor("PS", [P, 8, T], F32))

        x_in_s, par_s = sem("x_loaded"), sem("par_loaded")
        raw_s = [sem("raw0_loaded"), sem("raw1_loaded")]
        hi_s, lo_s = sem("hi_ready"), sem("lo_ready")
        tile_s = sem("tile_done")
        evac_s = sem("tile_evacuated")
        h_s, g_s = sem("h_ready"), sem("g_ready")
        sq_s, ss_s, rt_s = sem("squares"), sem("sumsq_used"), sem("root_ready")
        ones_s = sem("ones_ready")
        v_chain, a_chain = sem("v_chain"), sem("a_chain")
        ct_s, sg_s = sem("ct_ready"), sem("silu_ready")
        x_s = sem("x_final")
        out_s = sem("out_stored")
        ada_s = [sem("ada0_loaded"), sem("ada1_loaded")]
        mod_sum, mod_done = sem("mod_sums"), sem("mod_done")
        eps_s, cs_s = sem("eps_ready"), sem("cond_ready")
        ada_acc_s = sem("ada_acc")

        const_s = sem("const_loaded")
        vt_t, vt_s = sem("v_transposed"), sem("v_ready")
        gw_s, gt_t, gt_s = sem("gate_weights"), sem("gate_tile"), sem("gates_ready")
        w1_s, rw_s = [sem("w1k_loaded"), sem("w1v_loaded")], [sem("rawk_loaded"), sem("rawv_loaded")]
        xj_s, xj_used = sem("cmp_rows"), sem("cmp_rows_used")
        hid_s, kvc_t, kvc_s = sem("cmp_hidden"), sem("cmp_tile"), sem("cmp_ready")
        dist_s = sem("dist_loaded")
        sc_t, sc_m, sc_e, sc_n = sem("cmp_scores"), sem("cmp_shifted"), sem("cmp_exp"), sem("cmp_norm")
        pc_t, pc_s, oc_t, oc_s = sem("cmpT_tile"), sem("cmpT_ready"), sem("cmp_out_tile"), sem("cmp_out")
        stage_s, s_t, s_m, s_e, s_n = sem("staged"), sem("scores"), sem("shifted"), sem("exp"), sem("normalized")
        v_step = sem("v_step")
        xf_s, mask_s, gm_s = sem("first_block_done"), sem("masks_loaded"), sem("gain_ready")
        sq2_s, n2_t, r2_s, qk_s = sem("qk_squares"), sem("qk_sums"), sem("qk_root"), sem("qk_ready")
        vs_t, vs_e = sem("sv_transposed"), sem("sv_ready")
        ss_t, ss_x, ss_l, ss_c = sem("sb_logits"), sem("sb_masked"), sem("sb_log"), sem("sb_sums")
        ss_w, ss_e, st_t, st_s = sem("sb_diff"), sem("sb_weights"), sem("sbT_tile"), sem("sbT")
        so_t, so_s = sem("sb_out_tile"), sem("sb_out")
        ca_s, xb_s, dw_s = sem("conv_sum"), sem("xbc_rows"), sem("dt_weights")
        dt_t, dt_a, dt_e, dt_s = sem("dt_tile"), sem("dt_abs"), sem("dt_log"), sem("dt_ready")
        cs_t, ncs_s = sem("cumsum_tile"), sem("cumsum_ready")
        ch_s, xt_t, cb_t = sem("chunk_copied"), sem("chunk_turned"), sem("decay_rows")
        xdt_s, lm_s, ex_s = sem("xdt_ready"), sem("decay_shifted"), sem("exponents")
        le_s, de_s, mm_s = sem("decay_exp"), sem("exponents_exp"), sem("masked_scores")
        yd_t, y_s, yt_t, ck_s = sem("chunk_products"), sem("chunk_rows"), sem("chunk_outT"), sem("chunk_done")
        sz_s, sq3_s, z_t, rz_s = sem("silu_z"), sem("y_squares"), sem("y_sums"), sem("y_root")
        yo_s, ac_s = sem("ssd_out"), sem("adt_chunk")
        bias_s = sem("bias_ready")
        p_t, p_s, o_t, o_s = sem("probsT_tile"), sem("probsT"), sem("attn_tile"), sem("attn_out")
        col = {k: v for k, v in COL.items()}

        def pcol(name, j=0, n=1):
            return par[:, DS(col[name] + j, n)]

        block = ctx.enter_context(nc.Block())


        @block.sync
        def _(sp):
            def load_unit(seg, k, i):
                u = seg.unit0 + seg.upb * i + k
                if not (seg.unit0 + k < 2 and isinstance(i, int) and i == 0):
                    sp.wait_ge(lo_s, u - 1)
                src = streams[seg.kind][DS(seg.at0 + seg.upb * i + k, 1)]
                sp.dma_start(WR[:, k % 2, 0:seg.size], src.rearrange("a p n -> p (a n)")).then_inc(raw_s[k % 2], 16)

            def load_ada(n, slot):
                if not isinstance(n, int) or n >= 2:
                    sp.wait_ge(ada_acc_s, n - 1)
                sp.dma_start(AW[:, slot, :], wada[DS(n, 1)].rearrange("a p n -> p (a n)")).then_inc(ada_s[slot], 16)

            def segment(name, ada=None):
                seg = SEGS[name]

                def body(i):
                    for k in range(seg.upb):
                        load_unit(seg, k, i)
                        if ada is not None:
                            load_ada(ada + seg.upb * i + k, k % 2)
                if seg.unit0 == 0 or ada == 0:
                    body(0)
                    loop(sp, 1, seg.bodies, [], body)
                else:
                    loop(sp, 0, seg.bodies, [], body)

            sp.dma_start(par[:, :], par_in).then_inc(par_s, 16)
            sp.dma_start(ident[:, :], consts[:, 0:P]).then_inc(const_s, 16)
            sp.dma_start(bones[:, :], consts[:, P:2 * P]).then_inc(const_s, 16)
            sp.dma_start(slopes[:, :], consts[:, C_SLOPES:C_SLOPES + NH + 1]).then_inc(const_s, 16)
            sp.dma_start(X[:, :, :], x_in).then_inc(x_in_s, 16)
            for name, _, _ in SEGMENTS:
                segment(name, {"gu0a": 0, "gu1a": 12}.get(name))
            for m in range(DC):
                sp.wait_ge(x_s, m + 1)
                sp.dma_start(out[:, m, :], X[:, m, :]).then_inc(out_s, 16)
            sp.wait_ge(out_s, 16 * DC)


        @block.gpsimd
        def _(pool):
            nc.gpsimd.memset(ones[:, :], 1.0).then_inc(ones_s, 1)

            def segment(name):
                seg = SEGS[name]

                def body(i):
                    for k in range(seg.upb):
                        s, n = k % 2, seg.size
                        pool.wait_ge(hi_s, seg.unit0 + seg.upb * i + k + 1)
                        nc.gpsimd.tensor_tensor(WL[:, s, 0:n], WR[:, s, 0:n], WH[:, s, 0:n].bitcast(F32),
                                                ALU.subtract).then_inc(lo_s, 1)
                if name != "qkv":
                    loop(pool, 0, seg.bodies, [], body)
                    return

                def turn(r):
                    for b in range(3):
                        body(3 * r + b)

                    def steps(j):
                        for k in range(4):
                            w = P * k + P
                            pool.wait_ge(ss_c, 32 * r + 4 * j + k + 1)
                            nc.gpsimd.tensor_tensor(XM[:, k, 0:w], XM[:, k, 0:w], CC[:, k, 0:w],
                                                    ALU.subtract).then_inc(ss_w, 1)
                    loop(pool, 0, 8, [], steps)
                loop(pool, 0, 2, [], turn)

            for name, _, _ in SEGMENTS:
                segment(name)


        @block.tensor
        def _(pe):
            def dense(name, xh, xl, ready=None, after=None, only=None):
                seg = SEGS[name]

                def body(i, first=False):
                    for k in range(seg.upb):
                        s = k % 2
                        wh = WH[:, s, 0:seg.size].rearrange("p (c m) -> p c m", c=seg.chunks)
                        wl = WL[:, s, 0:seg.size].rearrange("p (c m) -> p c m", c=seg.chunks)
                        pe.wait_ge(lo_s, seg.unit0 + seg.upb * i + k + 1)
                        for m in range(seg.tiles):
                            b = k * seg.tiles + m
                            t = seg.tile0 + NB * i + b
                            if not isinstance(t, int) or t >= NB:
                                pe.wait_ge(evac_s, t - NB + 1)
                            cols = slice(m * P, m * P + P)
                            for c in range(seg.chunks):
                                if first and ready and b == 0:
                                    ready(c)
                                pe_h, pe_l = xh(c), xl(c)
                                nc.tensor.matmul(PS[:, b, :], wh[:, c, cols], pe_h, start=c == 0, stop=False)
                                nc.tensor.matmul(PS[:, b, :], wh[:, c, cols], pe_l, start=False, stop=False)
                                last = nc.tensor.matmul(PS[:, b, :], wl[:, c, cols], pe_h, start=False,
                                                        stop=c == seg.chunks - 1)
                            last.then_inc(tile_s, 1)
                            if after:
                                after(b)
                if only is not None:
                    body(only, ready is not None)
                    return
                body(0, True)
                loop(pe, 1, seg.bodies, [], body)

            def from_h(name, ready=None):
                dense(name, lambda c: Hh[:, c, :], lambda c: Hl[:, c, :], ready)

            def from_g(name, ready=None):
                dense(name, lambda c: Gh[:, c, :], lambda c: Gl[:, c, :], ready)

            norms = [0]

            def norm_stats():
                k = norms[0]
                norms[0] += 1

                for m in range(DC):
                    pe.wait_ge(sq_s, DC * k + m + 1)
                    nc.tensor.matmul(PS[:, 4, :], ones[:, :], SQ[:, m % 2, :], start=m == 0,
                                     stop=m == DC - 1).then_inc(ss_s, 1)

            def h_ready(c):
                pe.wait_ge(h_s, DC * hs[0] + c + 1)

            def g_ready(c):
                pe.wait_ge(g_s, gs[0] + c + 1)
            hs, gs = [0], [0]

            def feed_forward(l):
                norm_stats()
                for r, (half, n) in enumerate((("a", F1), ("b", F2))):
                    from_h(f"gu{l}{half}", h_ready if r == 0 else None)
                    if r == 0:
                        hs[0] += 1
                        if l < 2:
                            mod_sums(l)
                    from_g(f"dn{l}{half}", g_ready)
                    gs[0] += n

            def mod_sums(l):
                pe.wait_ge(ada_acc_s, 12 * (l + 1))
                if l:
                    pe.wait_ge(mod_done, 1)
                for n in range(24):
                    mm = nc.tensor.matmul(PS[:, 5, n:n + 1], AACC[:, n * P:n * P + P], ones[:, 0:1],
                                          start=True, stop=True)
                mm.then_inc(mod_sum, 1)

            pe.wait_ge(ones_s, 1)
            norm_stats()
            from_h("win", h_ready)
            hs[0] += 1
            from_g("wout", g_ready)
            gs[0] += DC
            feed_forward(0)
            def turn_values():
                end = SEGS["wkv"].tile0 + 12
                pe.wait_ge(evac_s, end)
                pe.wait_ge(const_s, 48)
                for n, (br, a) in enumerate(((0, 0), (0, 1), (1, 0), (1, 1))):
                    if n >= 2:
                        pe.wait_ge(vt_s, n - 1)
                    for kb in range(QB):
                        mm = nc.tensor.transpose(PS[:, 5 + n % 2, kb * P:kb * P + P],
                                                 KV[:, 6 + 4 * br + a, kb * P:kb * P + P], ident[:, :])
                    mm.then_inc(vt_t, 1)

            def gate_products():
                pe.wait_ge(gw_s, 1)
                for qb in range(QB):
                    o = PS[:, 7, qb * 3 * NH:(qb + 1) * 3 * NH]
                    tok = slice(qb * P, qb * P + P)
                    for c in range(DC):
                        nc.tensor.matmul(o, Hh[:, c, tok], GWH[:, c, :], start=c == 0, stop=False)
                        nc.tensor.matmul(o, Hl[:, c, tok], GWH[:, c, :], start=False, stop=False)
                        mm = nc.tensor.matmul(o, Hh[:, c, tok], GWL[:, c, :], start=False, stop=c == DC - 1)
                mm.then_inc(gt_t, 1)

            def compress():
                for s in range(2):
                    pe.wait_ge(w1_s[s], 16)
                    if s:
                        pe.wait_ge(hid_s, 2)
                    for j in range(16):
                        pe.wait_ge(xj_s, 16 * s + j + 1)
                        for mc in range(2):
                            mm = nc.tensor.matmul(PS[:, 4 + mc, 0:4 * CG], W1[s][:, j, mc * P:mc * P + P],
                                                  XJ[:, j % 2, :, :].rearrange("p g n -> p (g n)"),
                                                  start=j == 0, stop=j == 15)
                        mm.then_inc(xj_used, 1)
                    pe.wait_ge(hid_s, 2 * s + 2)
                    if s == 0:
                        w2 = pcol("w2k", 0, 256).rearrange("p (c m) -> p c m", c=2)
                        for mc in range(2):
                            mm = nc.tensor.matmul(PS[:, 6, 0:4 * CG], w2[:, mc, :],
                                                  HID[:, mc, :, :].rearrange("p g n -> p (g n)"),
                                                  start=mc == 0, stop=mc == 1)
                    else:
                        w2 = pcol("w2v", 0, 128).rearrange("p (c m) -> p c m", c=2)
                        pe.wait_ge(kvc_s, 1)
                        for g in range(4):
                            for mc in range(2):
                                rows = HIDR[:, mc, g, :, :].rearrange("p r n -> p (r n)")
                                mm = nc.tensor.matmul(PS[:, 6, g * HD:(g + 1) * HD], rows, w2[:, mc, :],
                                                      start=mc == 0, stop=mc == 1)
                    mm.then_inc(kvc_t, 1)

            def compressed_attention():
                pe.wait_ge(kvc_s, 2)
                pe.wait_ge(evac_s, SEGS["wq"].tile0 + DC)
                for qb in range(QB):
                    if qb:
                        pe.wait_ge(sc_m, qb)
                    for h in range(NH):
                        g, j = h // 4, h % 4
                        half = slice(HD * (g % 2), HD * (g % 2) + HD)
                        o = PS[:, 4 + g % 2, (g // 2) * P + j * CG:(g // 2) * P + j * CG + CG]
                        mm = nc.tensor.matmul(o, QT[half, 4 * (g // 2) + j, qb * P:qb * P + P],
                                              KC[half, g * CG:g * CG + CG], start=True, stop=True)
                    mm.then_inc(sc_t, 1)
                    pe.wait_ge(sc_n, qb + 1)
                    if qb:
                        pe.wait_ge(pc_s, qb)
                    for g in range(4):
                        mm = nc.tensor.transpose(PS[:, 6, g * P:g * P + P], SE[:, g * P:g * P + P], ident[:, :])
                    mm.then_inc(pc_t, 1)
                pe.wait_ge(pc_s, QB)
                for pair in range(DC):
                    b = pair % 4
                    if pair >= 4:
                        pe.wait_ge(oc_s, pair - 3)
                    j = pair % 4
                    for hf in range(2):
                        g = 2 * (pair // 4) + hf
                        mm = nc.tensor.matmul(PS[HD * hf:HD * hf + HD, b, :], VC[CG * j:CG * j + CG, g, :],
                                              PCT[CG * j:CG * j + CG, g, :], start=True, stop=True)
                    mm.then_inc(oc_t, 1)

            def attention():
                pe.wait_ge(oc_s, DC)

                def turn(first, base, kv_tile):
                    def step_of(k):
                        return k // 16, k // 8 % 2, k // 4 % 2, k % 4

                    for k in range(32 + 4):
                        if k < 32:
                            pp, hf, br, qb = step_of(k)
                            half = slice(HD * hf, HD * hf + HD)
                            if k % 16 == 0:
                                pe.wait_ge(stage_s, base(3) + pp + 2)
                            if k >= 3:
                                pe.wait_ge(s_m, base(32) + k - 2)
                            elif not first:
                                pe.wait_ge(s_m, base(32))
                            nc.tensor.matmul(PS[:, 4 + k % 3, 0:P * qb + P], QS[half, pp, qb * P:qb * P + P],
                                             kv_tile(half, 4 + 4 * br, P * qb + P), start=True, stop=True)\
                                .then_inc(s_t, 1)
                        if 3 <= k < 35:
                            pp, hf, br, qb = step_of(k - 3)
                            pe.wait_ge(s_n, base(32) + k - 2)
                            if k > 3 or not first:
                                pe.wait_ge(p_s, base(32) + k - 3)
                            for kb in range(qb + 1):
                                mm = nc.tensor.transpose(PS[:, 7, kb * P:kb * P + P],
                                                         PB[:, (k - 3) % 4, kb * P:kb * P + P], ident[:, :])
                            mm.then_inc(p_t, 1)
                        if k >= 4 and (k - 4) % 4 == 3:
                            pp, hf, br, _ = step_of(k - 4)
                            n = (k - 4) // 4
                            pe.wait_ge(p_s, base(32) + k - 3)
                            if n % 4 == 0 and not first:
                                pe.wait_ge(o_s, base(2) + pp)
                            for kb in range(QB):
                                mm = nc.tensor.matmul(PS[HD * hf:HD * hf + HD, pp, kb * P:T],
                                                      VS[:, br, kb, HD * hf:HD * hf + HD],
                                                      PT[:, n % 2, kb, kb * P:T], start=br == 0 and kb == 0,
                                                      stop=br == 1 and kb == QB - 1)
                            mm.then_inc(o_t, 1)

                for kt in range(2):
                    def keys(half, tile, n):
                        return KV[half, tile + kt, 0:n]
                    if kt == 0:
                        turn(True, lambda k: 0, keys)
                        loop(pe, 1, 2, [], lambda i: turn(False, lambda k: k, keys))
                    else:
                        loop(pe, 2, 4, [], lambda i: turn(False, lambda k: k * i, keys))

            norm_stats()
            from_h("wkv", h_ready)
            hs[0] += 1
            turn_values()
            from_h("wq", h_ready)
            hs[0] += 1
            gate_products()
            compress()
            compressed_attention()
            attention()
            dense("wo", lambda c: Hh[:, c, :], lambda c: Hl[:, c, :], lambda c: pe.wait_ge(o_s, DC))
            feed_forward(1)
            def stick_breaking(r):
                def bones_product(n):
                    pe.wait_ge(sq2_s, 8 * r + n + 1)
                    nc.tensor.matmul(PS[:, 4 + n % 2, :], bones[:, :], SQ2[:, n % 2, :], start=True, stop=True)\
                        .then_inc(n2_t, 1)

                tile0 = SEGS["qkv"].tile0
                for b3 in range(3):
                    def after(b):
                        n = 4 * b3 + b
                        if 1 <= n <= 8:
                            bones_product(n - 1)
                    dense("qkv", lambda c: Hh[:, c, :], lambda c: Hl[:, c, :], after=after, only=3 * r + b3)
                for a in range(4):
                    pe.wait_ge(evac_s, tile0 + 12 * r + 9 + a)
                    if a >= 2:
                        pe.wait_ge(vs_e, 4 * r + a - 1)
                    for kb in range(QB):
                        mm = nc.tensor.transpose(PS[:, 6 + a % 2, kb * P:kb * P + P],
                                                 QKV[:, 8 + a, kb * P:kb * P + P], ident[:, :])
                    mm.then_inc(vs_t, 1)
                pe.wait_ge(qk_s, 8 * r + 8)
                pe.wait_ge(vs_e, 4 * r + 4)
                for k in range(32 + 5):
                    if k < 32:
                        a, hf, qb = k // 8, k // 4 % 2, k % 4
                        half = slice(HD * hf, HD * hf + HD)
                        if k >= 4:
                            pe.wait_ge(ss_x, 32 * r + k - 3)
                        nc.tensor.matmul(PS[:, 4 + k % 4, 0:P * qb + P], QKV[half, a, qb * P:qb * P + P],
                                         QKV[half, 4 + a, 0:P * qb + P], start=True, stop=True).then_inc(ss_t, 1)
                    if 4 <= k < 36:
                        m = k - 4
                        pe.wait_ge(ss_e, 32 * r + m + 1)
                        if m >= 2:
                            pe.wait_ge(st_s, 32 * r + m - 1)
                        for kb in range(m % 4 + 1):
                            mm = nc.tensor.transpose(PS[:, m % 2, kb * P:kb * P + P],
                                                     XM[:, m % 4, kb * P:kb * P + P], ident[:, :])
                        mm.then_inc(st_t, 1)
                    if k >= 5 and (k - 5) % 4 == 3:
                        h = (k - 5) // 4
                        a, hf = h // 2, h % 2
                        pe.wait_ge(st_s, 32 * r + 4 * h + 4)
                        if a >= 2 and hf == 0:
                            pe.wait_ge(so_s, 4 * r + a - 1)
                        for kb in range(QB):
                            mm = nc.tensor.matmul(PS[HD * hf:HD * hf + HD, 2 + a % 2, kb * P:T],
                                                  VTS[:, kb, a * P + HD * hf:a * P + HD * hf + HD],
                                                  PTS[h % 2][:, kb, kb * P:T], start=kb == 0, stop=kb == QB - 1)
                        mm.then_inc(so_t, 1)
                pe.wait_ge(so_s, 4 * r + 4)

            def dt_products():
                pe.wait_ge(dw_s, 1)
                for qb in range(QB):
                    o = PS[:, 7, qb * NH:qb * NH + NH]
                    tok = slice(qb * P, qb * P + P)
                    for c in range(DC):
                        nc.tensor.matmul(o, Hh[:, c, tok], DWH[:, c, :], start=c == 0, stop=False)
                        nc.tensor.matmul(o, Hl[:, c, tok], DWH[:, c, :], start=False, stop=False)
                        mm = nc.tensor.matmul(o, Hh[:, c, tok], DWL[:, c, :], start=False, stop=c == DC - 1)
                mm.then_inc(dt_t, 1)
                pe.wait_ge(dt_s, 1)
                nc.tensor.matmul(PS[:, 6, 0:QB * NH], TRI, ADT[:, :, :].rearrange("p q h -> p (q h)"),
                                 start=True, stop=True).then_inc(cs_t, 1)

            def ssd_chunk(c):
                pe.wait_ge(ch_s, c + 1)
                pe.wait_ge(ncs_s, 1)
                pe.wait_ge(ac_s, c + 1)
                for f in range(DC):
                    nc.tensor.transpose(PS[:, 2 + f // 4, (f % 4) * P:(f % 4) * P + P], CH[:, f, :], ident[:, :])
                for g in range(2):
                    nc.tensor.transpose(PS[:, 4, (2 + g) * P:(3 + g) * P], CH[:, 8 + g, :], ident[:, :])
                for g in range(2):
                    mm = nc.tensor.matmul(PS[:, 4, g * P:g * P + P], CH[:, 8 + g, :], CH[:, 10 + g, :],
                                          start=True, stop=True)
                mm.then_inc(xt_t, 1)
                for q in range(2):
                    if q:
                        pe.wait_ge(lm_s, 2 * c + 1)
                    for h in range(8):
                        w = ADTC[:, 8 * q + h:8 * q + h + 1].to_broadcast([P, P])
                        mm = nc.tensor.matmul(PS[:, h // 4, (h % 4) * P:(h % 4) * P + P], w, TRI,
                                              start=True, stop=True)
                    mm.then_inc(cb_t, 1)
                for g in range(2):
                    nc.tensor.matmul(PS[:, 5 + g, :], CH[:, 10 + g, :],
                                     PREV[:, 8 * g:8 * g + 8, :].rearrange("p h d -> p (h d)"), start=True, stop=True)
                for q in range(2):
                    pe.wait_ge(mm_s, 2 * c + q + 1)
                    for h in range(8 * q, 8 * q + 8):
                        nc.tensor.matmul(PS[:, 2 + q, (h % 8) * HD:(h % 8) * HD + HD], LM[:, h, :], XDT[:, h, :],
                                         start=True, stop=True)
                pe.wait_ge(xdt_s, c + 1)
                for g in range(2):
                    mm = nc.tensor.matmul(PS[:, g, :], BTK[:, g, :],
                                          XDD[:, 8 * g:8 * g + 8, :].rearrange("p h d -> p (h d)"),
                                          start=True, stop=True)
                mm.then_inc(yd_t, 1)
                pe.wait_ge(y_s, c + 1)
                for f in range(DC):
                    mm = nc.tensor.transpose(PS[:, 5 + f // 4, (f % 4) * P:(f % 4) * P + P],
                                             YC[:, 2 * f:2 * f + 2, :].rearrange("p h d -> p (h d)"), ident[:, :])
                mm.then_inc(yt_t, 1)

            def z_products():
                def sum_product(m):
                    pe.wait_ge(sq3_s, m + 1)
                    nc.tensor.matmul(PS[:, 5 + m // 4, :], ones[:, :], SQ3[:, m % 2, :], start=m % 4 == 0,
                                     stop=m % 4 == 3).then_inc(z_t, 1)
                for i in range(2):
                    def after(b):
                        if 4 * i + b:
                            sum_product(4 * i + b - 1)
                    dense("zg", lambda c: Hh[:, c, :], lambda c: Hl[:, c, :], after=after, only=i)
                sum_product(7)

            norm_stats()
            norm_stats()
            for c in range(DC):
                h_ready(c)
            hs[0] += 1
            loop(pe, 0, 2, [], stick_breaking)
            from_h("xbc")
            dt_products()
            ssd_chunk(0)
            loop(pe, 1, QB, [], ssd_chunk)
            pe.wait_ge(ck_s, QB)
            z_products()
            dense("wout2", lambda c: Hh[:, c, :] if c < DC else Gh[:, c - DC, :],
                  lambda c: Hl[:, c, :] if c < DC else Gl[:, c - DC, :],
                  lambda c: pe.wait_ge(yo_s, c + 1) if c < DC else None)
            norm_stats()
            from_h("gu2a", h_ready)
            from_g("dn2a", g_ready)
            gs[0] += F1
            from_h("gu2b")
            from_g("dn2b", g_ready)




        @block.scalar
        def _(act):
            chain = Tally(act, a_chain)
            sgs, norms = [0], [0]

            def hi(u, i=None, per=0, size=0):
                if u >= UNITS:
                    return
                s = u % 2
                if i is None:
                    n = UNIT_SIZE[u]
                    act.wait_ge(raw_s[s], 16 * (u // 2 + 1))
                    if u >= 2:
                        act.wait_ge(tile_s, TILES_AFTER[u - 2])
                else:
                    n = size
                    act.wait_ge(raw_s[s], 16 * (u // 2 + 1) + 8 * per * i)
                    act.wait_ge(tile_s, TILES_AFTER[u - 2] + NB * i)
                nc.scalar.activation(WH[:, s, 0:n], WR[:, s, 0:n], ACT.Copy).then_inc(hi_s, 1)

            def dense(name, evac=None, per_turn=()):
                seg = SEGS[name]

                def body(i):
                    dynamic = not isinstance(i, int)
                    for k in range(seg.upb):
                        if evac:
                            evac(i, k)
                        if dynamic:
                            hi(seg.unit0 + k + 2, i, seg.upb, seg.size)
                        else:
                            hi(seg.unit0 + seg.upb * i + k + 2)
                loop(act, 0, seg.bodies - 1, list(per_turn), body)
                body(seg.bodies - 1)

            def norm_stats(ready, eps):
                k = norms[0]
                norms[0] += 1

                def body(i):
                    for s in range(2):
                        m = 2 * i + s
                        ready(m)
                        if not (isinstance(i, int) and k == 0 and i == 0):
                            act.wait_ge(ss_s, DC * k + m - 1)
                        nc.scalar.activation(SQ[:, s, :], X[:, DS(m, 1), :].rearrange("p a t -> p (a t)"),
                                             ACT.Square).then_inc(sq_s, 1)
                if k == 0:
                    body(0)
                    loop(act, 1, DC // 2, [], body)
                else:
                    loop(act, 0, DC // 2, [], body)
                act.wait_ge(ss_s, DC * (k + 1))
                nc.scalar.activation(RT[:, :], PS[:, 4, :], ACT.Sqrt, scale=1.0 / D, bias=eps_col(eps))\
                    .then_inc(rt_s, 1)

            def eps_col(eps):
                return EPSC[:, 0:1] if eps == EPS1 else EPSC[:, 1:2]

            def feed_forward(l, ready, eps):
                norm_stats(ready, eps)
                for half, n in (("a", F1), ("b", F2)):
                    seg = SEGS[f"gu{l}{half}"]

                    def evac(i, k):
                        t = seg.tile0 + NB * i + 2 * k
                        act.wait_ge(tile_s, t + 1)
                        act.wait_ge(evac_s, t - 2)
                        nc.scalar.activation(SG[:, k, :], PS[:, 2 * k, :], ACT.Silu).then_inc(sg_s, 1)
                    dense(f"gu{l}{half}", evac)
                    dense(f"dn{l}{half}")

            def tiles_out(name):
                return lambda m: act.wait_ge(evac_s, SEGS[name].tile0 + m + 1)

            def conv_evac():
                seg = SEGS["win"]
                for u in range(seg.units):
                    for t in (2 * u, 2 * u + 1):
                        if t % 3 == 0:
                            j = t // 3
                            act.wait_ge(tile_s, t + 1)
                            if j >= 2:
                                act.wait_ge(evac_s, 3 * (j - 2) + 2)
                            nc.scalar.activation(CT[:, j % 2, :], PS[:, t % NB, :], ACT.Copy).then_inc(ct_s, 1)
                    hi(u + 2)

            act.wait_ge(par_s, 16)
            act.wait_ge(eps_s, 2)
            nc.scalar.activation(CSIL[:, :], pcol("cond", 0, 8), ACT.Silu).then_inc(cs_s, 1)
            hi(0)
            hi(1)
            act.wait_ge(x_in_s, 16)
            norm_stats(lambda m: None, EPS1)
            conv_evac()
            dense("wout")
            feed_forward(0, tiles_out("wout"), EPS1)
            def load_compression():
                act.wait_ge(evac_s, SEGS["wkv"].tile0 + 12)
                act.dma_start(W1[0][:, :, :], w1k.rearrange("p (j m) -> p j m", j=16)).then_inc(w1_s[0], 16)
                act.dma_start(W1[1][:, :, :], w1v.rearrange("p (j m) -> p j m", j=16)).then_inc(w1_s[1], 16)

            def load_raw(s):
                for g in range(4):
                    src = KV[HD * (g % 2):HD * (g % 2) + HD, 2 * s + g // 2, :]
                    act.dma_start(RW[0:HD, g, :], src).then_inc(rw_s[s], 16)
                    act.dma_start(RW[HD:P, g, 0:T - 1], src[:, 1:T]).then_inc(rw_s[s], 16)

            def compress():
                for s in range(2):
                    for mc in range(2):
                        act.wait_ge(xj_used, 16 * s + 16)
                        src = PS[:, 4 + mc, 0:4 * CG].rearrange("p (g n) -> p g n", g=4)
                        if s == 0:
                            nc.scalar.activation(HID[:, mc, :, :], src, ACT.Silu).then_inc(hid_s, 1)
                        else:
                            nc.scalar.activation(HIDR[:, mc, :, :, :],
                                                 src.unsqueeze(2).to_broadcast([P, 4, 4, CG]), ACT.Silu)\
                                .then_inc(hid_s, 1)
                    if s == 0:
                        load_raw(1)
                    act.wait_ge(kvc_t, s + 1)
                    if s == 0:
                        nc.scalar.activation(KC[:, :], PS[:, 6, 0:4 * CG], ACT.Copy).then_inc(kvc_s, 1)
                    else:
                        nc.scalar.activation(VC[:, :, :].rearrange("p g d -> p (g d)"), PS[:, 6, 0:4 * HD],
                                             ACT.Copy).then_inc(kvc_s, 1)
                act.wait_ge(rw_s[0], 128)
                act.wait_ge(rw_s[1], 128)
                act.dma_start(DIST[:, :], consts[:, C_DIST:C_DIST + T]).then_inc(dist_s, 16)
                act.dma_start(DISTC[:, :, :], consts[:, C_DISTC:C_DISTC + QB * CG].rearrange(
                    "p (a n) -> p a n", a=QB)).then_inc(dist_s, 16)

            def compressed_attention():
                for qb in range(QB):
                    act.wait_ge(sc_m, qb + 1)
                    nc.scalar.activation(SE[:, :], SC[:, :], ACT.Exp).then_inc(sc_e, 1)
                    act.wait_ge(pc_t, qb + 1)
                    nc.scalar.activation(PCT[:, :, qb * P:qb * P + P],
                                         PS[:, 6, :].rearrange("p (g q) -> p g q", g=4), ACT.Copy).then_inc(pc_s, 1)
                for pair in range(DC):
                    act.wait_ge(oc_t, pair + 1)
                    nc.scalar.activation(OC[:, pair, :], PS[:, pair % 4, :], ACT.Copy).then_inc(oc_s, 1)

            def attention():
                act.wait_ge(dist_s, 32)

                def turn(first, i, base):
                    def stage(pp):
                        if not first:
                            act.wait_ge(s_t, base(32))
                            act.wait_ge(s_m, base(32))
                        if not first and pp == 0:
                            act.wait_ge(o_t, base(8))
                        nc.scalar.activation(QS[:, pp, :], QT[:, DS(2 * i + pp, 1), :].rearrange("p a t -> p (a t)"),
                                             ACT.Copy).then_inc(stage_s, 1)
                        if pp == 0:
                            nc.scalar.activation(VS[:, :, :, :], VT[:, :, :, kt * P:kt * P + P], ACT.Copy)\
                                .then_inc(stage_s, 1)
                        for hf in range(2):
                            h = 8 * kt + 4 * hf + 2 * (i - 2 * kt) + pp
                            nc.scalar.activation(BIAS[:, 2 * pp + hf, :], DIST[:, :], ACT.Copy,
                                                 scale=slopes[:, DS(h, 1)]).then_inc(bias_s, 1)

                    stage(0)
                    for k in range(32 + 3):
                        if k == 8:
                            stage(1)
                        if k < 32:
                            act.wait_ge(s_m, base(32) + k + 1)
                            w = P * (k % 4) + P
                            nc.scalar.activation(PB[:, k % 4, 0:w], PB[:, k % 4, 0:w], ACT.Exp,
                                                 bias=NMX[:, 1, k:k + 1], accum_out=SMX[:, 0, k:k + 1])\
                                .then_inc(s_e, 1)
                        if k >= 3:
                            qb, n = (k - 3) % 4, (k - 3) // 4
                            act.wait_ge(p_t, base(32) + k - 2)
                            if n >= 2 or not first:
                                act.wait_ge(o_t, base(8) + n - 1)
                            nc.scalar.activation(PT[:, n % 2, 0:qb + 1, qb * P:qb * P + P],
                                                 PS[:, 7, 0:P * qb + P].rearrange("p (k q) -> p k q", q=P),
                                                 ACT.Copy).then_inc(p_s, 1)

                for kt in range(2):
                    if kt == 0:
                        turn(True, 0, lambda k: 0)
                        loop(act, 1, 2, [], lambda i: turn(False, i, lambda k: k * i))
                    else:
                        loop(act, 2, 4, [], lambda i: turn(False, i, lambda k: k * i))

            norm_stats(tiles_out("dn0b"), EPS1)
            dense("wkv")
            load_compression()
            load_raw(0)
            for n, (br, a) in enumerate(((0, 0), (0, 1), (1, 0), (1, 1))):
                act.wait_ge(vt_t, n + 1)
                nc.scalar.activation(VT[:, br, :, a * P:a * P + P],
                                     PS[:, 5 + n % 2, :].rearrange("p (k d) -> p k d", d=P), ACT.Copy)\
                    .then_inc(vt_s, 1)
            dense("wq")
            act.wait_ge(gt_t, 1)
            nc.scalar.activation(GT[:, :, :].rearrange("p q h -> p (q h)"), PS[:, 7, 0:3 * NH * QB], ACT.Sigmoid)\
                .then_inc(gt_s, 1)
            compress()
            compressed_attention()
            attention()
            dense("wo")
            feed_forward(1, tiles_out("wo"), EPS1)
            def stick_breaking(r):
                seg = SEGS["qkv"]

                def square(n):
                    act.wait_ge(evac_s, seg.tile0 + 12 * r + n + 1)
                    nc.scalar.activation(SQ2[:, n % 2, :], QKV[:, n, :], ACT.Square).then_inc(sq2_s, 1)

                def root(n):
                    act.wait_ge(n2_t, 8 * r + n + 1)
                    if n >= 2:
                        act.wait_ge(qk_s, 8 * r + n - 1)
                    nc.scalar.activation(RT2[:, n % 2, :], PS[:, 4 + n % 2, :], ACT.Sqrt, scale=1.0 / HD,
                                         bias=eps_col(EPS2)).then_inc(r2_s, 1)
                for u in range(6):
                    for n in (2 * u, 2 * u + 1):
                        if n < 8:
                            square(n)
                        if n % 2 == 0 and 1 <= n <= 8:
                            root(n - 1)
                    if isinstance(r, int):
                        hi(seg.unit0 + 6 * r + u + 2)
                    else:
                        hi(seg.unit0 + u % 2 + 2, 3 * r + u // 2, seg.upb, seg.size)
                    if u < 4:
                        root(2 * u)
                for a in range(4):
                    act.wait_ge(vs_t, 4 * r + a + 1)
                    nc.scalar.activation(VTS[:, :, a * P:a * P + P],
                                         PS[:, 6 + a % 2, :].rearrange("p (k d) -> p k d", d=P), ACT.Copy)\
                        .then_inc(vs_e, 1)
                for k in range(32 + 4):
                    if k < 32:
                        w = P * (k % 4) + P
                        act.wait_ge(ss_x, 32 * r + k + 1)
                        chain.mark(nc.scalar.activation(EE[:, k % 4, 0:w], EE[:, k % 4, 0:w], ACT.Exp))
                        chain.wait()
                        nc.scalar.activation(EE[:, k % 4, 0:w], EE[:, k % 4, 0:w], ACT.Ln, bias=1.0)\
                            .then_inc(ss_l, 1)
                    if 2 <= k < 34:
                        m = k - 2
                        w = P * (m % 4) + P
                        act.wait_ge(ss_w, 32 * r + m + 1)
                        nc.scalar.activation(XM[:, m % 4, 0:w], XM[:, m % 4, 0:w], ACT.Exp).then_inc(ss_e, 1)
                    if k >= 4:
                        m = k - 4
                        qb, h = m % 4, m // 4
                        act.wait_ge(st_t, 32 * r + m + 1)
                        if h >= 2:
                            act.wait_ge(so_t, 8 * r + h - 1)
                        nc.scalar.activation(PTS[h % 2][:, 0:qb + 1, qb * P:qb * P + P],
                                             PS[:, m % 2, 0:P * qb + P].rearrange("p (k q) -> p k q", q=P),
                                             ACT.Copy).then_inc(st_s, 1)

            def dt_log():
                act.wait_ge(dt_a, 2)
                flat = DTE[:, :, :].rearrange("p q h -> p (q h)")
                chain.mark(nc.scalar.activation(flat, flat, ACT.Exp))
                chain.wait()
                nc.scalar.activation(flat, flat, ACT.Ln, bias=1.0).then_inc(dt_e, 1)
                nc.scalar.activation(AN[:, :], pcol("alog", 0, NH), ACT.Exp).then_inc(dt_e, 1)

            def ssd_chunk(c):
                if not (isinstance(c, int) and c == 0):
                    act.wait_ge(ck_s, c)
                nc.scalar.activation(CH[:, :, :], XB[:, :, DS(P * c, P)], ACT.Copy).then_inc(ch_s, 1)
                for q in range(2):
                    act.wait_ge(lm_s, 2 * c + q + 1)
                    for h in range(8 * q, 8 * q + 8):
                        ins = nc.scalar.activation(LM[:, h, :], LM[:, h, :], ACT.Exp,
                                                   bias=NCS[:, DS(c, 1), h:h + 1].rearrange("p a h -> p (a h)"))
                    ins.then_inc(le_s, 1)
                act.wait_ge(ex_s, c + 1)
                nc.scalar.activation(EX[:, :, :], EX[:, :, :], ACT.Exp).then_inc(de_s, 1)

            def z_evac():
                seg = SEGS["zg"]

                def root(g):
                    act.wait_ge(z_t, 4 * g + 4)
                    nc.scalar.activation(RZ[:, g, :], PS[:, 5 + g, :], ACT.Sqrt, scale=2.0 / D,
                                         bias=eps_col(EPS2)).then_inc(rz_s, 1)
                for u in range(4):
                    for m in (2 * u, 2 * u + 1):
                        act.wait_ge(tile_s, seg.tile0 + m + 1)
                        if m >= 2:
                            act.wait_ge(evac_s, seg.tile0 + m - 1)
                        nc.scalar.activation(SZ[:, m % 2, :], PS[:, m % NB, :], ACT.Silu).then_inc(sz_s, 1)
                        act.wait_ge(evac_s, seg.tile0 + m + 1)
                        if m >= 2:
                            act.wait_ge(z_t, m - 1)
                        nc.scalar.activation(SQ3[:, m % 2, :], XB[:, m, :], ACT.Square).then_inc(sq3_s, 1)
                    hi(seg.unit0 + u + 2)
                for g in range(2):
                    root(g)

            act.wait_ge(gw_s, 1)
            act.wait_ge(o_s, DC)
            act.dma_start(par[:, COL["gatew"]:COL["gatew"] + 3 * P], consts[:, C_TRI:C_TRI + 3 * P])\
                .then_inc(mask_s, 16)
            norm_stats(tiles_out("dn1b"), EPS1)
            norm_stats(lambda m: act.wait_ge(xf_s, m + 1), EPS2)
            loop(act, 0, 2, [(chain, 32)], stick_breaking)

            def silu_xbc(i, k):
                for m in range(2):
                    t = 4 * i + 2 * k + m
                    act.wait_ge(ca_s, t + 1)
                    nc.scalar.activation(XB[:, DS(t, 1), :].rearrange("p a t -> p (a t)"), CA[:, m, :], ACT.Silu)\
                        .then_inc(xb_s, 1)
            dense("xbc", silu_xbc)
            dt_log()
            ssd_chunk(0)
            loop(act, 1, QB, [], ssd_chunk)
            z_evac()
            dense("wout2")
            feed_forward(2, tiles_out("wout2"), EPS2)




        @block.vector
        def _(dve):
            chain = Tally(dve, v_chain)
            norms, sgs, ada_n = [0], [0], [0]

            def row(tensor, m):
                return tensor[:, DS(m, 1), :].rearrange("p a t -> p (a t)")

            def split(dst_h, dst_l, src, sem_):
                chain.mark(nc.vector.tensor_copy(dst_h, src))
                chain.wait()
                nc.vector.tensor_tensor(dst_l, src, dst_h.bitcast(F32), ALU.subtract).then_inc(sem_, 1)

            def norm(gain, shift=None, to_x=None, again=None):
                if again:
                    dve.wait_ge(tile_s, again)
                else:
                    norms[0] += 1
                    dve.wait_ge(rt_s, norms[0])
                    chain.mark(nc.vector.reciprocal(RS[:, :], RT[:, :]))
                    chain.wait()
                hs = h_count[0]

                def body(i):
                    for s in range(2):
                        m = 2 * i + s
                        if to_x:
                            nc.vector.scalar_tensor_tensor(row(X, m), row(X, m), gain(m), RS[:, :], ALU.mult,
                                                           ALU.mult).then_inc(to_x, 1)
                            continue
                        dve.wait_ge(h_s, hs + m - 1) if not (isinstance(i, int) and hs + m < 2) else None
                        chain.mark(nc.vector.scalar_tensor_tensor(XN[:, s, :], row(X, m), gain(m), RS[:, :],
                                                                  ALU.mult, ALU.mult))
                        chain.wait()
                        if shift:
                            chain.mark(nc.vector.tensor_scalar(XN[:, s, :], XN[:, s, :], shift(m), None, ALU.add))
                            chain.wait()
                        split(row(Hh, m), row(Hl, m), XN[:, s, :], h_s)
                per = 0 if to_x else (6 if shift else 4)
                if hs == 0:
                    body(0)
                    loop(dve, 1, DC // 2, [(chain, per)], body)
                else:
                    loop(dve, 0, DC // 2, [(chain, per)], body)
                if not to_x:
                    h_count[0] += DC

            h_count, g_count = [0], [0]

            def conv_mixer():
                for j in range(DC):
                    t = 3 * j
                    dve.wait_ge(ct_s, j + 1)
                    dve.wait_ge(tile_s, t + 2)
                    nc.vector.tensor_tensor(CV[:, 2:T + 2], CT[:, j % 2, :], PS[:, (t + 1) % NB, :],
                                            ALU.mult).then_inc(evac_s, 2)
                    dve.wait_ge(evac_s, t + 2)
                    for tap in range(3):
                        w = pcol("conv1", 8 * tap + j)
                        if tap == 0:
                            chain.mark(nc.vector.tensor_scalar(CU[:, :], CV[:, 0:T], w, None, ALU.mult))
                        else:
                            chain.mark(nc.vector.scalar_tensor_tensor(CU[:, :], CV[:, tap:T + tap], w, CU[:, :],
                                                                      ALU.mult, ALU.add))
                        chain.wait()
                    dve.wait_ge(tile_s, t + 3)
                    if j:
                        dve.wait_ge(g_s, j)
                    nc.vector.tensor_tensor(HT[:, :], CU[:, :], PS[:, (t + 2) % NB, :], ALU.mult)\
                        .then_inc(evac_s, 1)
                    dve.wait_ge(evac_s, t + 3)
                    split(Gh[:, j, :], Gl[:, j, :], HT[:, :], g_s)
                g_count[0] += DC

            def residual(name, scale=None):
                seg = SEGS[name]

                def body(i):
                    for b in range(NB):
                        m = NB * i + b
                        dve.wait_ge(tile_s, seg.tile0 + m + 1)
                        if scale is None:
                            ins = nc.vector.tensor_tensor(row(X, m), row(X, m), PS[:, b, :], ALU.add)
                        else:
                            ins = nc.vector.scalar_tensor_tensor(row(X, m), PS[:, b, :], scale(m), row(X, m),
                                                                 ALU.mult, ALU.add)
                        ins.then_inc(evac_s, 1)
                loop(dve, 0, DC // NB, [], body)

            def feed_forward(l, gain, shift=None, scale=None, ada=None):
                norm(gain, shift)
                for half, n in (("a", F1), ("b", F2)):
                    seg = SEGS[f"gu{l}{half}"]
                    g0, s0, with_ada = g_count[0], sgs[0], half == "a" and ada is not None

                    def body(i):
                        for k in range(2):
                            f = 2 * i + k
                            t = seg.tile0 + NB * i + 2 * k
                            dve.wait_ge(sg_s, s0 + f + 1)
                            dve.wait_ge(tile_s, t + 2)
                            dve.wait_ge(g_s, g0 + f)
                            nc.vector.tensor_tensor(HF[:, :], SG[:, k, :], PS[:, 2 * k + 1, :], ALU.mult)\
                                .then_inc(evac_s, 2)
                            dve.wait_ge(evac_s, t + 2)
                            split(row(Gh, f), row(Gl, f), HF[:, :], g_s)
                            if with_ada:
                                modulation_unit(ada + f, f, k)
                    loop(dve, 0, n // 2, [(chain, 2 + (14 if with_ada else 0))], body)
                    g_count[0] += n
                    sgs[0] += n
                    if with_ada:
                        dve.wait_ge(mod_sum, l + 1)
                        nc.vector.tensor_tensor(MOD[:, 24 * l:24 * l + 24], PS[:, 5, 0:24],
                                                pcol("bada", 24 * l, 24), ALU.add).then_inc(mod_done, 1)
                    residual(f"dn{l}{half}", scale)

            def modulation_unit(n, f, slot):
                dve.wait_ge(ada_s[slot], 8 * n - 8 * slot + 16)
                acc = AACC[:, DS(256 * f, 256)]
                for c in range(DC):
                    w = AW[:, slot, c * 256:c * 256 + 256]
                    if c == 0:
                        chain.mark(nc.vector.tensor_scalar(acc, w, CSIL[:, 0:1], None, ALU.mult))
                        chain.wait()
                    elif c < DC - 1:
                        chain.mark(nc.vector.scalar_tensor_tensor(acc, w, CSIL[:, c:c + 1], acc, ALU.mult, ALU.add))
                        chain.wait()
                    else:
                        nc.vector.scalar_tensor_tensor(acc, w, CSIL[:, c:c + 1], acc, ALU.mult, ALU.add)\
                            .then_inc(ada_acc_s, 1)

            nc.vector.memset(EPSC[:, 0:1], EPS1).then_inc(eps_s, 1)
            nc.vector.memset(EPSC[:, 1:2], EPS2).then_inc(eps_s, 1)
            chain.mark(nc.vector.memset(CV[:, 0:2], 0.0))
            chain.wait()
            dve.wait_ge(par_s, 16)
            dve.wait_ge(cs_s, 1)
            dve.wait_ge(x_in_s, 16)
            norm(lambda m: pcol("a_norm", m))
            conv_mixer()
            residual("wout")
            feed_forward(0, lambda m: pcol("f_norm0", m), ada=0)
            def copy_tiles(name, dst, turns, scale=None):
                seg = SEGS[name]

                def body(i):
                    for b in range(NB):
                        n = NB * i + b
                        dve.wait_ge(tile_s, seg.tile0 + n + 1)
                        if scale is None:
                            nc.vector.tensor_copy(dst(n), PS[:, b, :]).then_inc(evac_s, 1)
                        else:
                            nc.vector.tensor_scalar(dst(n), PS[:, b, :], scale, None, ALU.mult).then_inc(evac_s, 1)
                loop(dve, 0, turns, [], body)

            def compress_rows():
                dve.wait_ge(vt_s, 4)
                for r in range(2):
                    chain.mark(nc.vector.memset(XJ[:, r, :, :], 0.0))
                chain.wait()
                for s in range(2):
                    dve.wait_ge(rw_s[s], 128)
                    for j in range(16):
                        if 16 * s + j >= 2:
                            dve.wait_ge(xj_used, 16 * s + j - 1)
                        nc.vector.tensor_scalar(XJ[:, j % 2, :, 0:NCMP], RW[:, :, 2 * j:2 * j + 16 * (NCMP - 1) + 1:16],
                                                pcol("pek" if s == 0 else "pev", j), None, ALU.add)\
                            .then_inc(xj_s, 1)

            def compressed_attention():
                dve.wait_ge(dist_s, 32)
                dve.wait_ge(gt_s, 1)

                def heads(x):
                    return x.rearrange("p (h n) -> p h n", n=CG)

                def wide(x):
                    return x.unsqueeze(2).to_broadcast([P, NH, CG])
                for qb in range(QB):
                    if qb:
                        dve.wait_ge(sc_e, qb)
                    chain.mark(nc.vector.tensor_tensor(
                        heads(CB[:, :]), DISTC[:, qb, :].unsqueeze(1).to_broadcast([P, NH, CG]),
                        wide(slopes[:, 0:NH]), ALU.mult))
                    chain.wait()
                    dve.wait_ge(sc_t, qb + 1)
                    chain.mark(nc.vector.tensor_tensor(
                        SC[:, :].rearrange("p (a b x) -> p a b x", a=2, b=2),
                        CB[:, :].rearrange("p (a b x) -> p a b x", a=2, b=2),
                        PS[:, 4:6, 0:2 * P].rearrange("p b (a x) -> p a b x", a=2), ALU.add))
                    chain.wait()
                    chain.mark(nc.vector.tensor_reduce(CMX[:, 0, :], heads(SC[:, :]), AX_X, ALU.max))
                    chain.wait()
                    nc.vector.tensor_tensor(heads(SC[:, :]), heads(SC[:, :]), wide(CMX[:, 0, :]), ALU.subtract)\
                        .then_inc(sc_m, 1)
                    dve.wait_ge(sc_e, qb + 1)
                    chain.mark(nc.vector.tensor_reduce(CMX[:, 1, :], heads(SE[:, :]), AX_X, ALU.add))
                    chain.wait()
                    chain.mark(nc.vector.reciprocal(CMX[:, 2, :], CMX[:, 1, :]))
                    chain.wait()
                    gate = GT[:, qb, 0:3 * NH:3]
                    if qb == 0:
                        chain.mark(nc.vector.scalar_tensor_tensor(CMX[:, 1, :], CMX[:, 2, :], visrow, gate,
                                                                  ALU.mult, ALU.mult))
                    else:
                        chain.mark(nc.vector.tensor_tensor(CMX[:, 1, :], CMX[:, 2, :], gate, ALU.mult))
                    chain.wait()
                    if qb:
                        dve.wait_ge(pc_t, qb)
                    nc.vector.tensor_tensor(heads(SE[:, :]), heads(SE[:, :]), wide(CMX[:, 1, :]), ALU.mult)\
                        .then_inc(sc_n, 1)

            def attention():
                def turn(first, i, base):
                    def shift(k):
                        pp, hf, qb = k // 16, k // 8 % 2, k % 4
                        w = P * qb + P
                        dve.wait_ge(s_t, base(32) + k + 1)
                        dve.wait_ge(bias_s, base(4) + 2 * pp + hf + 1)
                        if k >= 4 or not first:
                            dve.wait_ge(p_t, base(32) + k - 3)
                        if not isinstance(i, int):
                            dve.sem_inc(v_step, 1)
                        chain.mark(nc.vector.tensor_tensor_reduce(
                            out=PB[:, k % 4, 0:w], in0=PS[:, 4 + k % 3, 0:w], in1=BIAS[:, 2 * pp + hf, T - w:T],
                            scale=1.0, scalar=-3.0e38, op0=ALU.add, op1=ALU.max, accum_out=NMX[:, 0, k:k + 1]))
                        chain.wait()
                        nc.vector.tensor_scalar(NMX[:, 1, k:k + 1], NMX[:, 0, k:k + 1], -1.0, None, ALU.mult)\
                            .then_inc(s_m, 1)

                    def scale(k):
                        pp, hf, br, qb = k // 16, k // 8 % 2, k // 4 % 2, k % 4
                        w = P * qb + P
                        dve.wait_ge(s_e, base(32) + k + 1)
                        chain.mark(nc.vector.reciprocal(SMX[:, 1, k:k + 1], SMX[:, 0, k:k + 1]))
                        chain.wait()
                        h = 8 * kt + 4 * hf + 2 * (i - 2 * kt) + pp
                        gate = GT[:, qb, DS(3 * h + 1 + br, 1)]
                        nc.vector.tensor_scalar(PB[:, k % 4, 0:w], PB[:, k % 4, 0:w], SMX[:, 1, k:k + 1], gate,
                                                ALU.mult, ALU.mult).then_inc(s_n, 1)

                    def out_pair(pp):
                        pair = 2 * i + pp
                        dve.wait_ge(o_t, base(8) + 4 * pp + 4)
                        chain.mark(nc.vector.tensor_tensor(XO[:, :], row(OC, pair), PS[:, pp, :], ALU.add))
                        chain.wait()
                        split(row(Hh, pair), row(Hl, pair), XO[:, :], o_s)
                        dve.wait_ge(o_s, base(2) + pp + 1)

                    for k in range(32 + 1):
                        if k < 32:
                            shift(k)
                        if k:
                            scale(k - 1)
                        if k == 23:
                            out_pair(0)
                    out_pair(1)

                per = 32 + 32 + 2 * 2
                for kt in range(2):
                    if kt == 0:
                        turn(True, 0, lambda k: 0)
                        loop(dve, 1, 2, [(chain, per)], lambda i: turn(False, i, lambda k: k * i))
                    else:
                        loop(dve, 2, 4, [(chain, per)], lambda i: turn(False, i, lambda k: k * i))

            kv_end = SEGS["wkv"].tile0 + 12
            norm(lambda m: pcol("kv_norm", m))
            copy_tiles("wkv", lambda n: row(KV, n), 3)
            norm(lambda m: pcol("b_norm", m), again=kv_end)
            dve.wait_ge(vt_s, 4)
            chain.mark(nc.vector.tensor_copy(GWH[:, :, :].rearrange("p c m -> p (c m)"), pcol("gatew", 0, 384)))
            chain.wait()
            nc.vector.tensor_tensor(GWL[:, :, :].rearrange("p c m -> p (c m)"), pcol("gatew", 0, 384),
                                    GWH[:, :, :].rearrange("p c m -> p (c m)").bitcast(F32), ALU.subtract)\
                .then_inc(gw_s, 1)
            copy_tiles("wq", lambda n: row(QT, n), 2, HD ** -0.5)
            compress_rows()
            compressed_attention()
            attention()
            residual("wo")
            feed_forward(1, lambda m: pcol("f_norm1", m), ada=12)
            def stick_breaking(r):
                seg = SEGS["qkv"]

                def normalize(n):
                    dve.wait_ge(r2_s, 8 * r + n + 1)
                    chain.mark(nc.vector.reciprocal(RT2[:, n % 2, :], RT2[:, n % 2, :]))
                    chain.wait()
                    nc.vector.scalar_tensor_tensor(QKV[:, n, :], QKV[:, n, :], pcol("qn" if n < 4 else "kn"),
                                                   RT2[:, n % 2, :], ALU.mult, ALU.mult).then_inc(qk_s, 1)
                for n in range(12):
                    dve.wait_ge(tile_s, seg.tile0 + 12 * r + n + 1)
                    nc.vector.tensor_copy(QKV[:, n, :], PS[:, n % NB, :]).then_inc(evac_s, 1)
                    if 2 <= n < 10:
                        normalize(n - 2)

                def logits(k):
                    w = P * (k % 4) + P
                    dve.wait_ge(ss_t, 32 * r + k + 1)
                    if k >= 4:
                        dve.wait_ge(st_t, 32 * r + k - 3)
                    if k % 4:
                        chain.mark(nc.vector.tensor_scalar(XM[:, k % 4, 0:w - P], PS[:, 4 + k % 4, 0:w - P],
                                                           HD ** -0.5, None, ALU.mult))
                    chain.mark(nc.vector.scalar_tensor_tensor(XM[:, k % 4, w - P:w], PS[:, 4 + k % 4, w - P:w],
                                                              HD ** -0.5, MASK, ALU.mult, ALU.add))
                    chain.wait()
                    nc.vector.scalar_tensor_tensor(EE[:, k % 4, 0:w], XM[:, k % 4, 0:w], -1.0,
                                                   XM[:, k % 4, 0:w], ALU.mult, ALU.min).then_inc(ss_x, 1)

                def sums(k):
                    w = P * (k % 4) + P
                    dve.wait_ge(ss_l, 32 * r + k + 1)
                    chain.mark(nc.vector.scalar_tensor_tensor(EE[:, k % 4, 0:w], XM[:, k % 4, 0:w], 0.0,
                                                              EE[:, k % 4, 0:w], ALU.max, ALU.add))
                    chain.wait()
                    if k >= 4:
                        dve.wait_ge(ss_w, 32 * r + k - 3)
                    nc.vector.tensor_tensor_scan(CC[:, k % 4, 0:w][:, ::-1], ones[:, 0:1].to_broadcast([P, w]),
                                                 EE[:, k % 4, 0:w][:, ::-1], 0.0, ALU.mult, ALU.add)\
                        .then_inc(ss_c, 1)

                def out_pair(a):
                    dve.wait_ge(so_t, 8 * r + 2 * a + 2)
                    split(row(Gh, 4 * r + a), row(Gl, 4 * r + a), PS[:, 2 + a % 2, :], so_s)
                for k in range(33):
                    if k < 32:
                        logits(k)
                    if k:
                        sums(k - 1)
                    if k % 8 == 6 and k > 8:
                        out_pair(k // 8 - 1)
                out_pair(3)

            def conv_xbc():
                seg = SEGS["xbc"]

                def body(i):
                    for b in range(NB):
                        t = NB * i + b
                        dve.wait_ge(tile_s, seg.tile0 + t + 1)
                        nc.vector.tensor_copy(RB[:, 3:T + 3], PS[:, b, :]).then_inc(evac_s, 1)
                        dve.wait_ge(evac_s, seg.tile0 + t + 1)
                        if not isinstance(i, int) or t >= 2:
                            dve.wait_ge(xb_s, t - 1)
                        acc = CA[:, b % 2, :]
                        chain.mark(nc.vector.tensor_scalar(acc, RB[:, 0:T], pcol("conv2", t),
                                                           pcol("conv2b", t), ALU.mult, ALU.add))
                        chain.wait()
                        for tap in range(1, 4):
                            ins = nc.vector.scalar_tensor_tensor(acc, RB[:, tap:T + tap], pcol("conv2", 12 * tap + t),
                                                                 acc, ALU.mult, ALU.add)
                            if tap < 3:
                                chain.mark(ins)
                                chain.wait()
                            else:
                                ins.then_inc(ca_s, 1)
                                dve.wait_ge(ca_s, t + 1)
                body(0)
                loop(dve, 1, 3, [(chain, 12)], body)

            def dt_rows():
                dve.wait_ge(dt_t, 1)
                flat = "p q h -> p (q h)"
                bias = pcol("dtb", 0, NH).unsqueeze(1).to_broadcast([P, QB, NH])
                nc.vector.tensor_tensor(DT[:, :, :], PS[:, 7, 0:QB * NH].rearrange("p (q h) -> p q h", q=QB), bias,
                                        ALU.add).then_inc(dt_a, 1)
                dve.wait_ge(dt_a, 1)
                nc.vector.scalar_tensor_tensor(DTE[:, :, :].rearrange(flat), DT[:, :, :].rearrange(flat), -1.0,
                                               DT[:, :, :].rearrange(flat), ALU.mult, ALU.min).then_inc(dt_a, 1)
                dve.wait_ge(dt_e, 2)
                chain.mark(nc.vector.scalar_tensor_tensor(DT[:, :, :].rearrange(flat), DT[:, :, :].rearrange(flat), 0.0,
                                                          DTE[:, :, :].rearrange(flat), ALU.max, ALU.add))
                chain.wait()
                nc.vector.scalar_tensor_tensor(ADT[:, :, :], DT[:, :, :], -1.0,
                                               AN[:, :].unsqueeze(1).to_broadcast([P, QB, NH]), ALU.mult,
                                               ALU.mult).then_inc(dt_s, 1)
                dve.wait_ge(cs_t, 1)
                chain.mark(nc.vector.tensor_copy(CS[:, :, :].rearrange(flat), PS[:, 6, 0:QB * NH]))
                chain.mark(nc.vector.memset(PREV[:, :, :], 0.0))
                chain.wait()
                nc.vector.tensor_scalar(NCS[:, :, :].rearrange(flat), CS[:, :, :].rearrange(flat), -1.0, None,
                                        ALU.mult).then_inc(ncs_s, 1)

            def ssd_chunk(c):
                def small(x):
                    return x[:, DS(c, 1), :].rearrange("p a h -> p (a h)")

                def per_head(x):
                    return x.unsqueeze(2).to_broadcast([P, NH, HD])

                def bank_rows(b):
                    return PS[:, b:b + 2, :].rearrange("p b (h d) -> p (b h) d", d=HD)
                nc.vector.tensor_copy(ADTC[:, :], small(ADT)).then_inc(ac_s, 1)
                dve.wait_ge(xt_t, c + 1)
                chain.mark(nc.vector.tensor_tensor(XDT[:, :, :], bank_rows(2), per_head(small(DT)), ALU.mult))
                chain.mark(nc.vector.tensor_copy(SCR[:, :, :].rearrange("p g l -> p (g l)"), PS[:, 4, 0:2 * P]))
                chain.mark(nc.vector.tensor_copy(BTK[:, :, :].rearrange("p g l -> p (g l)"), PS[:, 4, 2 * P:4 * P]))
                for q in range(2):
                    dve.wait_ge(cb_t, 2 * c + q + 1)
                    chain.mark(nc.vector.tensor_copy(CSL[:, 8 * q:8 * q + 8].rearrange("p (b h) -> p b h", b=2),
                                                     PS[:, 0:2, P - 1:4 * P:P]))
                    nc.vector.tensor_tensor(LM[:, 8 * q:8 * q + 8, :],
                                            PS[:, 0:2, :].rearrange("p b (h l) -> p (b h) l", l=P),
                                            MASKL.unsqueeze(1).to_broadcast([P, 8, P]), ALU.add).then_inc(lm_s, 1)
                chain.wait()
                chain.mark(nc.vector.tensor_tensor(EX[:, 0, :], CSL[:, :], small(CS), ALU.subtract))
                chain.mark(nc.vector.tensor_copy(EX[:, 1, :], CSL[:, :]))
                nc.vector.tensor_copy(EX[:, 2, :], small(CS)).then_inc(ex_s, 1)
                for q in range(2):
                    dve.wait_ge(le_s, 2 * c + q + 1)
                    nc.vector.tensor_tensor(LM[:, 8 * q:8 * q + 8, :], LM[:, 8 * q:8 * q + 8, :],
                                            SCR[:, q, :].unsqueeze(1).to_broadcast([P, 8, P]), ALU.mult)\
                        .then_inc(mm_s, 1)
                dve.wait_ge(de_s, c + 1)
                nc.vector.tensor_tensor(XDD[:, :, :], XDT[:, :, :], per_head(EX[:, 0, :]), ALU.mult)\
                    .then_inc(xdt_s, 1)
                dve.wait_ge(yd_t, c + 1)
                chain.mark(nc.vector.tensor_tensor(YC[:, :, :], bank_rows(5), per_head(EX[:, 2, :]), ALU.mult))
                chain.mark(nc.vector.tensor_tensor(PREV[:, :, :], PREV[:, :, :], per_head(EX[:, 1, :]), ALU.mult))
                chain.wait()
                nc.vector.tensor_tensor(YC[:, :, :], YC[:, :, :], bank_rows(2), ALU.add).then_inc(y_s, 1)
                chain.mark(nc.vector.tensor_tensor(PREV[:, :, :], PREV[:, :, :], bank_rows(0), ALU.add))
                chain.wait()
                dve.wait_ge(yt_t, c + 1)
                for f in range(DC):
                    xs = XB[:, f, DS(P * c, P)]
                    ins = nc.vector.scalar_tensor_tensor(xs, xs, pcol("dskip", f),
                                                         PS[:, 5 + f // 4, (f % 4) * P:(f % 4) * P + P],
                                                         ALU.mult, ALU.add)
                ins.then_inc(ck_s, 1)
                dve.wait_ge(ck_s, c + 1)

            def gated_rows():
                seg = SEGS["zg"]
                for m in range(DC):
                    dve.wait_ge(sz_s, m + 1)
                    nc.vector.tensor_tensor(XB[:, m, :], XB[:, m, :], SZ[:, m % 2, :], ALU.mult).then_inc(evac_s, 1)
                dve.wait_ge(tile_s, seg.tile0 + DC)
                for g in range(2):
                    dve.wait_ge(rz_s, g + 1)
                    chain.mark(nc.vector.reciprocal(RZ[:, g, :], RZ[:, g, :]))
                    chain.wait()
                    for m in range(4 * g, 4 * g + 4):
                        if m >= 2:
                            dve.wait_ge(yo_s, m - 1)
                        chain.mark(nc.vector.scalar_tensor_tensor(XN2[:, m % 2, :], XB[:, m, :], pcol("ssdn", m),
                                                                  RZ[:, g, :], ALU.mult, ALU.mult))
                        chain.wait()
                        split(Hh[:, m, :], Hl[:, m, :], XN2[:, m % 2, :], yo_s)

            def gain_of(weight, scale):
                chain.mark(nc.vector.scalar_tensor_tensor(GM[:, :], MOD[:, scale:scale + DC], 1.0, pcol(weight, 0, DC),
                                                          ALU.add, ALU.mult))
                chain.wait()

            norm(lambda m: pcol("final", m), to_x=xf_s)
            dve.wait_ge(mod_done, 2)
            dve.wait_ge(xf_s, DC)
            gain_of("norm1", 8)
            norm(lambda m: GM[:, DS(m, 1)], shift=lambda m: MOD[:, DS(m, 1)])
            dve.wait_ge(mask_s, 16)
            loop(dve, 0, 2, [(chain, 8 + 32 + 24 + 32 + 4)], stick_breaking)
            dve.wait_ge(so_s, DC)
            dtw = pcol("dtw", 0, 128)
            chain.mark(nc.vector.tensor_copy(DWH[:, :, :].rearrange("p c h -> p (c h)"), dtw))
            chain.mark(nc.vector.memset(RB[:, 0:3], 0.0))
            chain.wait()
            nc.vector.tensor_tensor(DWL[:, :, :].rearrange("p c h -> p (c h)"), dtw,
                                    DWH[:, :, :].rearrange("p c h -> p (c h)").bitcast(F32), ALU.subtract)\
                .then_inc(dw_s, 1)
            conv_xbc()
            dt_rows()
            ssd_chunk(0)
            loop(dve, 1, QB, [(chain, 3 + 2 + 2 + 2 + 1)], ssd_chunk)
            gated_rows()
            residual("wout2", lambda m: MOD[:, DS(16 + m, 1)])
            gain_of("norm2", 32)
            feed_forward(2, lambda m: GM[:, DS(m, 1)], shift=lambda m: MOD[:, DS(24 + m, 1)],
                         scale=lambda m: MOD[:, DS(40 + m, 1)])
            dve.wait_ge(evac_s, TILES_AFTER[-1])
            dve.sem_inc(x_s, DC)




def kernel(**inputs):
    import numpy as np
    import concourse.bacc as bacc
    from concourse.bass_utils import run_bass_kernel_spmd as run

    a = {k: np.asarray(v) for k, v in inputs.items()}

    def tiles(w, chunks=None):
        k, m = w.shape
        return w.reshape(k // P, P, m // P, P).transpose(2, 1, 0, 3)

    def units(t, n):
        u = t.reshape(t.shape[0] // n, n, *t.shape[1:])
        return u.transpose(0, 2, 3, 1, 4).reshape(u.shape[0], P, -1)

    w_in = tiles(a["a_w_in"][0]).reshape(3, DC, P, DC, P)
    w_in = w_in[[1, 2, 0]].transpose(1, 0, 2, 3, 4).reshape(3 * DC, P, DC, P)
    kinds = {k: [] for k in KINDS}

    def ff(gate, up, down):
        g, u = tiles(gate), tiles(up)
        pair = np.stack([g, u], 1).reshape(2 * FC, P, DC, P)
        dn = tiles(down)
        kinds["A"].append(units(pair, 2))
        kinds["B"].append(units(dn[:, :, 0:F1], 1))
        kinds["C"].append(units(dn[:, :, F1:FC], 1))

    f_gu, f_dn = a["f_w_gu"], a["f_w_down"]
    kinds["A"] += [units(w_in, 2), units(tiles(a["a_w_out"][0]), 2)]
    ff(f_gu[0][:, :F], f_gu[0][:, F:], f_dn[0])
    kinds["A"].append(units(tiles(a["w_kv"]), 2))
    order = [8 * p + j + 4 * h for p in range(2) for j in range(4) for h in range(2)]
    qg = a["b_w_qg"][0]
    wq = qg[:, :NH * HD].reshape(D, NH, HD)[:, order].reshape(D, NH * HD)
    kinds["A"].append(units(tiles(wq), 2))
    wo = a["b_w_o"][0].reshape(NH, HD, D)[order].reshape(NH * HD, D)
    kinds["A"].append(units(tiles(wo), 2))
    ff(f_gu[1][:, :F], f_gu[1][:, F:], f_dn[1])
    wi = a["w_in_2"][0]
    z, xbc, dtw, q, k, v = (wi[:, lo:hi] for lo, hi in
                            ((0, 1024), (1024, 2560), (2560, 2576), (2576, 3600), (3600, 4624), (4624, 5648)))
    q, k, v = tiles(q), tiles(k), tiles(v)
    for r in range(2):
        kinds["A"].append(units(np.concatenate([w[4 * r:4 * r + 4] for w in (q, k, v)]), 2))
    kinds["A"] += [units(tiles(xbc), 2), units(tiles(z), 2)]
    kinds["D"].append(units(tiles(a["w_out_2"][0]), 1))
    ff(a["w_gate_2"][0], a["w_up_2"][0], a["w_down_2"][0])

    def cols(w):
        return w.reshape(-1, P).T

    def rows(w, n):
        return w.reshape(n, P, -1).transpose(1, 0, 2).reshape(P, -1)

    def wide(w):
        return np.broadcast_to(w[None, :], (P, w.shape[0]))

    w2k = rows(np.concatenate([a["cmp_w2_k"]] * 2, 1), 2)
    par = {
        "a_norm": cols(a["a_norm"][0]), "f_norm0": cols(a["f_norm"][0]), "kv_norm": cols(a["kv_norm"]),
        "b_norm": cols(a["b_norm"][0]), "f_norm1": cols(a["f_norm"][1]), "final": cols(a["final_norm"]),
        "norm1": cols(a["norm1_w_2"][0]), "norm2": cols(a["norm2_w_2"][0]),
        "conv1": cols(a["a_conv"][0].reshape(-1)), "conv2": cols(a["conv_w_2"][0].reshape(-1)),
        "conv2b": cols(a["conv_b_2"][0]), "ssdn": cols(a["ssd_norm_w_2"][0]),
        "dskip": cols(np.broadcast_to(a["d_skip_2"][0][:, None], (NH, HD)).reshape(-1)),
        "qn": cols(np.concatenate([a["q_norm_w_2"][0]] * 2)), "kn": cols(np.concatenate([a["k_norm_w_2"][0]] * 2)),
        "bada": cols(a["b_ada_2"][0]), "cond": cols(a["c_2"][0]),
        "pek": cols(a["cmp_pe_k"].reshape(-1)), "pev": cols(a["cmp_pe_v"].reshape(-1)),
        "dtb": wide(a["dt_bias_2"][0]), "alog": wide(a["a_log_2"][0]),
        "gatew": rows(qg[:, NH * HD:], DC), "dtw": rows(dtw, DC), "w2k": w2k, "w2v": rows(a["cmp_w2_v"], 2),
    }
    for n, w in PARAMS:
        assert par[n].shape == (P, w), (n, par[n].shape, w)
    arrays = {
        "x_in": a["x"][0].reshape(T, DC, P).transpose(2, 1, 0),
        **{f"w{k}": np.concatenate(v) for k, v in kinds.items()},
        "wada": units(tiles(a["w_ada_2"][0]), 2),
        "w1k": rows(a["cmp_w1_k"], 16), "w1v": rows(a["cmp_w1_v"], 16),
        "par": np.concatenate([par[n] for n, _ in PARAMS], 1),
    }
    p, y = np.arange(P)[:, None], np.arange(T)[None, :]
    dist = np.where(y > p + T - P, BIG, p + T - P - y)
    qb, n = np.arange(QB)[None, :, None], np.arange(CG)[None, None, :]
    tok = p[:, :, None] + P * qb
    distc = np.where(16 * n + 31 > tok, BIG, tok - 16 * n - 15.5).reshape(P, -1)
    c = np.zeros((P, C_END), np.float32)
    c[:, C_IDENT:C_IDENT + P] = p == y[:, :P]
    c[:, C_BONES:C_BONES + P] = p // HD == y[:, :P] // HD
    c[:, C_SLOPES:C_SLOPES + NH] = -np.exp2(-8.0 * np.arange(1, NH + 1) / NH)[None, :]
    c[:, C_VIS:C_VIS + 1] = p >= 31
    c[:, C_DIST:C_DIST + T] = dist
    c[:, C_DISTC:C_DISTC + QB * CG] = distc
    c[:, C_TRI:C_TRI + P] = p <= y[:, :P]
    c[:, C_MASKL:C_MASKL + P] = np.where(p <= y[:, :P], 0.0, -BIG)
    c[:, C_MASK:C_MASK + P] = np.where(y[:, :P] < p, 0.0, -BIG)
    arrays["consts"] = c
    nc = bacc.Bacc("TRN2", target_bir_lowering=False, num_devices=1)
    arrays = {k: np.ascontiguousarray(v) for k, v in arrays.items()}
    args = [nc.dram_tensor(k, v.shape, F32, kind="ExternalInput").ap() for k, v in arrays.items()]
    out = nc.dram_tensor("out", (P, DC, T), F32, kind="ExternalOutput").ap()
    two_blocks(nc, *args, out)
    got = run(nc, [arrays], core_ids=[0]).results[0]["out"]
    return np.ascontiguousarray(got.transpose(2, 1, 0).reshape(1, T, D))
```

```python
from contextlib import ExitStack

import concourse.bass as bass
from concourse import mybir

F32 = mybir.dt.float32
F32R = mybir.dt.float32r
ALU = mybir.AluOpType
ACT = mybir.ActivationFunctionType
AX_X = mybir.AxisListType.X

P = 128
T = 512
D = 1024
DC = D // P
F = 2816
FC = F // P
F1, F2 = 12, 10
NB = 4
KMAX = 2048
QB = T // P
HD = 64
NH = 16
NCMP = 31
CG = 32
BIG = 3.0e30
EPS1 = 1e-5
EPS2 = 1e-6
DS = bass.ds

SEGMENTS = [
    ("win", "A", 12), ("wout", "A", 4),
    ("gu0a", "A", F1), ("dn0a", "B", 8), ("gu0b", "A", F2), ("dn0b", "C", 8),
    ("wkv", "A", 6), ("wq", "A", 4), ("wo", "A", 4),
    ("gu1a", "A", F1), ("dn1a", "B", 8), ("gu1b", "A", F2), ("dn1b", "C", 8),
    ("qkv", "A", 12), ("xbc", "A", 6), ("wog", "A", 4), ("zg", "A", 4), ("woh", "A", 4),
    ("gu2a", "A", F1), ("dn2a", "B", 8), ("gu2b", "A", F2), ("dn2b", "C", 8),
]
KINDS = {"A": (DC, 2), "B": (F1, 1), "C": (F2, 1)}


class Segment:

    def __init__(self, name, kind, units, unit0, tile0, at0):
        self.name, self.kind, self.units = name, kind, units
        self.chunks, self.tiles = KINDS[kind]
        self.size = self.chunks * self.tiles * P
        self.unit0, self.tile0, self.at0 = unit0, tile0, at0
        self.upb = NB // self.tiles
        self.bodies = units // self.upb


def plan():
    segs, unit, tile, at = {}, 0, 0, {k: 0 for k in KINDS}
    size, after = [], []
    for name, kind, units in SEGMENTS:
        s = segs[name] = Segment(name, kind, units, unit, tile, at[kind])
        assert s.bodies * s.upb == units
        for u in range(units):
            size.append(s.size)
            after.append(tile + s.tiles * (u + 1))
        unit, tile, at[kind] = unit + units, tile + s.tiles * units, at[kind] + units
    return segs, size, after


SEGS, UNIT_SIZE, TILES_AFTER = plan()
UNITS = len(UNIT_SIZE)

PARAMS = [("a_norm", 8), ("f_norm0", 8), ("kv_norm", 8), ("b_norm", 8), ("f_norm1", 8), ("final", 8),
          ("norm1", 8), ("norm2", 8), ("conv1", 24), ("conv2", 48), ("conv2b", 12), ("ssdn", 8),
          ("dskip", 8), ("qn", 1), ("kn", 1), ("bada", 48), ("cond", 8), ("pek", 16), ("pev", 16),
          ("dtb", 16), ("alog", 16), ("gatew", 384), ("dtw", 128), ("w2k", 256), ("w2v", 128)]
COL, _n = {}, 0
for _name, _w in PARAMS:
    COL[_name] = _n
    _n += _w
NPAR = _n


C_IDENT, C_BONES, C_SLOPES, C_VIS = 0, P, 2 * P, 2 * P + NH
C_DIST = C_VIS + 1
C_DISTC = C_DIST + T
C_TRI = C_DISTC + QB * CG
C_MASK = C_TRI + P
C_MASKL = C_MASK + P
C_END = C_MASKL + P


class Tally:

    def __init__(self, eng, sem):
        self.eng, self.sem, self.n, self.var = eng, sem, 0, 0

    def mark(self, ins, by=1):
        ins.then_inc(self.sem, by)
        self.n += by

    def wait(self):
        self.eng.wait_ge(self.sem, self.var + self.n if not isinstance(self.var, int) else self.n)


def loop(eng, first, last, tallies, body):
    if last - first == 1:
        body(first)
        return
    if last <= first:
        return
    with eng.Fori(first, last) as i:
        start = [t.n for t, _ in tallies]
        outer = [t.var for t, _ in tallies]
        for t, k in tallies:
            t.var = t.var + (i - first) * k
        body(i)
        for (t, k), n, var in zip(tallies, start, outer):
            assert t.n - n == k, (t.n - n, k)
            t.var = var
            t.n = n + k * (last - first)


def two_blocks(nc, x_in, wA, wB, wC, wada, w1k, w1v, par_in, consts, out):
    streams = {"A": wA, "B": wB, "C": wC}
    ctx = ExitStack()
    with ctx:
        arena0 = (nc.sbuf_base + 31) // 32 * 32
        KB = 1024
        ctx.enter_context(nc.sbuf_tensor("arena", [P, 207 * KB + 512], mybir.dt.uint8))

        def at(name, kb, shape, dt=F32):
            size = 4
            for n in shape[1:]:
                size *= n
            assert kb * KB + size <= 207.5 * KB, name
            return nc.alloc_sbuf_tensor_at(name, shape, dt, offset=arena0 + int(kb * KB))

        def sem(name):
            return ctx.enter_context(nc.semaphore(name))

        X = at("X", 0, [P, DC, T])
        Hh = at("Hh", 16, [P, DC, T], F32R)
        Hl = at("Hl", 32, [P, DC, T], F32R)
        Gh = at("Gh", 48, [P, F1, T], F32R)
        Gl = at("Gl", 72, [P, F1, T], F32R)
        WR = at("WR", 96, [P, 2, KMAX])
        WH = at("WH", 112, [P, 2, KMAX], F32R)
        WL = at("WL", 128, [P, 2, KMAX], F32R)
        SQ = at("SQ", 144, [P, 2, T])
        RS = at("RS", 150, [P, T])
        XN = at("XN", 152, [P, 3, T])
        ACC = at("ACC", 158, [P, T])
        par = at("par", 200, [P, NPAR])
        ones = at("ones", 205, [P, P])
        EPSC = at("EPSC", 205.75, [P, 2])
        CSIL = at("CSIL", 205.8125, [P, DC])
        MOD = at("MOD", 205.5, [P, 48])
        CT = at("CT", 156, [P, 2, T])
        CV = at("CV", 160, [P, T + 8])
        CU = at("CU", 163, [P, T])
        HT = at("HT", 196, [P, T])
        SG = at("SG", 160, [P, 2, T])
        HF = at("HF", 164, [P, T])
        AW = at("AW", 166, [P, 2, KMAX])
        AACC = at("AACC", 182, [P, 24 * P])

        KV = at("KV", 48, [P, 12, T])
        QT = at("QT", 72, [P, DC, T])
        VT = at("VT", 88, [P, 2, QB, 256])
        OC = at("OC", 144, [P, DC, T])
        W1 = [at("W1K", 160, [P, 16, 256]), at("W1V", 176, [P, 16, 256])]
        RW = [at("RWK", 192, [P, 4, T]), at("RWV", 80, [P, 4, T])]
        XJ = at("XJ", 144, [P, 2, 16, 4, CG])
        HID = at("HID", 61, [P, 2, 4, CG])
        HIDR = at("HIDR", 192, [P, 2, 4, 4, CG])
        KC = at("KC", 62, [P, 2, 2, CG])
        VC = at("VC", 63, [P, 4, HD])
        GT = at("GT", 68, [P, QB, 3 * NH])
        GWH = at("GWH", 144, [P, DC, P], F32R)
        GWL = at("GWL", 148, [P, DC, P], F32R)
        GO = at("GO", 54, [P, T])
        DIST = at("DIST", 48, [P, T])
        XO = at("XO", 50, [P, T])
        NMX = at("NMX", 52, [P, 2, 32])
        SMX = at("SMX", 52.5, [P, 2, 32])
        DISTC = at("DISTC", 53, [P, QB, CG])
        CMX = at("CMX", 53.5, [P, 3, NH])
        SC = at("SC", 176, [P, 2, T])
        CB = at("CB", 180, [P, T])
        SE = at("SE", 182, [P, 2, T])
        PCT = at("PCT", 192, [P, 4, T])
        PT = at("PT", 160, [P, 2, QB, T])
        PB = at("PB", 176, [P, 6, T])
        BIAS = at("BIAS", 188, [P, 4, T])
        QS = at("QS", 196, [P, 2, T])
        QKV = at("QKV", 144, [P, 12, T])
        VTS = at("VTS", 168, [P, QB, T])
        SQ2 = at("SQ2", 176, [P, 2, T])
        RT2 = at("RT2", 180, [P, 2, T])
        XM = at("XM", 180, [P, 3, T])
        MW = at("MW", 186, [P, T])
        EE = at("EE", 176, [P, 2, T])
        CC = at("CC", 188, [P, 6, T])
        PTS = [at("PTSa", 64, [P, QB, T]), at("PTSb", 88, [P, QB, T])]
        XB = at("XB", 144, [P, 12, T])
        RB = at("RB", 168, [P, T + 8])
        CA = at("CA", 171, [P, 2, T])
        CH = at("CH", 168, [P, 12, P])
        XDT = at("XDT", 174, [P, NH, HD])
        XDD = at("XDD", 178, [P, NH, HD])
        LM = at("LM", 182, [P, NH, P])
        YC = at("YC", 190, [P, NH, HD])
        PREV = at("PREV", 194, [P, NH, HD])
        BTK = at("BTK", 198, [P, 2, P])
        SCR = at("SCR", 199, [P, 2, P])
        DT = at("DT", 64, [P, QB, NH])
        DTE = at("DTE", 64.25, [P, QB, NH])
        ADT = at("ADT", 64.5, [P, QB, NH])
        CS = at("CS", 64.75, [P, QB, NH])
        NCS = at("NCS", 65, [P, QB, NH])
        EX = at("EX", 65.25, [P, 3, NH])
        CSL = at("CSL", 65.5, [P, NH])
        AN = at("AN", 65.625, [P, NH])
        ADTC = at("ADTC", 65.75, [P, NH])
        DWH = at("DWH", 88, [P, DC, P], F32R)
        DWL = at("DWL", 92, [P, DC, P], F32R)
        DTR = at("DTR", 176, [P, T])
        SZ = at("SZ", 168, [P, 2, T])
        SQ3 = at("SQ3", 172, [P, 2, T])
        RZ = at("RZ", 176, [P, 2, T])
        XN2 = at("XN2", 180, [P, 2, T])
        GM = at("GM", 205.6875, [P, DC])
        ident = at("ident", 206, [P, P])
        bones = at("bones", 206.5, [P, P])
        slopes = at("slopes", 207, [P, NH + 1])
        visrow = slopes[:, NH:NH + 1]

        gw = COL["gatew"]
        TRI, MASK, MASKL = par[:, gw:gw + P], par[:, gw + P:gw + 2 * P], par[:, gw + 2 * P:gw + 3 * P]
        PS = ctx.enter_context(nc.psum_tensor("PS", [P, 8, T], F32))

        x_in_s, par_s = [sem(f"x{m}_loaded") for m in range(DC)], sem("par_loaded")
        raw_s = [sem("raw0_loaded"), sem("raw1_loaded")]
        hi_s, lo_s = sem("hi_ready"), sem("lo_ready")
        tile_s = sem("tile_done")
        evac_s = sem("tile_evacuated")
        h_s, g_s = sem("h_ready"), sem("g_ready")
        sq_s, ss_s, rt_s = sem("squares"), sem("squares_added"), sem("root_ready")
        mean_t, xn_s, hh_s = sem("mean_tile"), sem("normalized_chunk"), sem("h_high")
        ones_s = sem("ones_ready")
        v_chain, a_chain = sem("v_chain"), sem("a_chain")
        ct_s, sg_s = sem("ct_ready"), sem("silu_ready")
        out_s = sem("out_stored")
        ada_s = [sem("ada0_loaded"), sem("ada1_loaded")]
        mod_sum, mod_done = sem("mod_sums"), sem("mod_done")
        eps_s, cs_s = sem("eps_ready"), sem("cond_ready")
        ada_acc_s = sem("ada_acc")

        const_s = sem("const_loaded")
        vt_t, vt_s = sem("v_transposed"), sem("v_ready")
        gt_r, dt_r, go_s, dr_s = sem("gate_rows"), sem("dt_rows"), sem("gate_rows_out"), sem("dt_rows_out")
        gw_s, gt_t, gt_s = sem("gate_weights"), sem("gate_tile"), sem("gates_ready")
        w1_s, rw_s = [sem("w1k_loaded"), sem("w1v_loaded")], [sem("rawk_loaded"), sem("rawv_loaded")]
        xj_s, xj_used = sem("cmp_rows"), sem("cmp_rows_used")
        hid_s, kvc_t, kvc_s = sem("cmp_hidden"), sem("cmp_tile"), sem("cmp_ready")
        dist_s = sem("dist_loaded")
        sc_t, sc_m, sc_e, sc_n = sem("cmp_scores"), sem("cmp_shifted"), sem("cmp_exp"), sem("cmp_norm")
        pc_t, pc_s, oc_t, oc_s = sem("cmpT_tile"), sem("cmpT_ready"), sem("cmp_out_tile"), sem("cmp_out")
        stage_s, s_t, s_m, s_e, s_n = sem("staged"), sem("scores"), sem("shifted"), sem("exp"), sem("normalized")
        v_step = sem("v_step")
        xf_s, mask_s = sem("first_block_done"), sem("masks_loaded")
        sq2_s, n2_t, r2_s, qk_s = sem("qk_squares"), sem("qk_sums"), sem("qk_root"), sem("qk_ready")
        vs_t, vs_e = sem("sv_transposed"), sem("sv_ready")
        ss_t, ss_x, ss_l, ss_c = sem("sb_logits"), sem("sb_masked"), sem("sb_log"), sem("sb_sums")
        ss_w, ss_e, st_t, st_s = sem("sb_diff"), sem("sb_weights"), sem("sbT_tile"), sem("sbT")
        so_t, so_s = sem("sb_out_tile"), sem("sb_out")
        ca_s, xb_s, dw_s = sem("conv_sum"), sem("xbc_rows"), sem("dt_weights")
        dt_t, dt_a, dt_e, dt_s = sem("dt_tile"), sem("dt_abs"), sem("dt_log"), sem("dt_ready")
        cs_t, ncs_s = sem("cumsum_tile"), sem("cumsum_ready")
        ch_s, xt_t, cb_t = sem("chunk_copied"), sem("chunk_turned"), sem("decay_rows")
        xdt_s, lm_s, ex_s = sem("xdt_ready"), sem("decay_shifted"), sem("exponents")
        le_s, de_s, mm_s = sem("decay_exp"), sem("exponents_exp"), sem("masked_scores")
        yd_t, y_s, yt_t, ck_s = sem("chunk_products"), sem("chunk_rows"), sem("chunk_outT"), sem("chunk_done")
        sz_s, sq3_s, z_t, rz_s = sem("silu_z"), sem("y_squares"), sem("y_sums"), sem("y_root")
        yo_s, ac_s = sem("ssd_out"), sem("adt_chunk")
        bias_s = sem("bias_ready")
        p_t, p_s, o_t, o_s = sem("probsT_tile"), sem("probsT"), sem("attn_tile"), sem("attn_out")
        col = {k: v for k, v in COL.items()}

        def pcol(name, j=0, n=1):
            return par[:, DS(col[name] + j, n)]

        block = ctx.enter_context(nc.Block())


        @block.sync
        def _(sp):
            def load_unit(seg, k, i):
                u = seg.unit0 + seg.upb * i + k
                if not (seg.unit0 + k < 2 and isinstance(i, int) and i == 0):
                    sp.wait_ge(lo_s, u - 1)
                src = streams[seg.kind][DS(seg.at0 + seg.upb * i + k, 1)]
                sp.dma_start(WR[:, k % 2, 0:seg.size], src.rearrange("a p n -> p (a n)")).then_inc(raw_s[k % 2], 16)

            def load_ada(n, slot):
                if not isinstance(n, int) or n >= 2:
                    sp.wait_ge(ada_acc_s, n - 1)
                sp.dma_start(AW[:, slot, :], wada[DS(n, 1)].rearrange("a p n -> p (a n)")).then_inc(ada_s[slot], 16)

            def segment(name, ada=None):
                seg = SEGS[name]

                def body(i):
                    for k in range(seg.upb):
                        load_unit(seg, k, i)
                        if ada is not None:
                            load_ada(ada + seg.upb * i + k, k % 2)
                if seg.unit0 == 0 or ada == 0:
                    body(0)
                    loop(sp, 1, seg.bodies, [], body)
                else:
                    loop(sp, 0, seg.bodies, [], body)

            for m in range(DC):
                sp.dma_start(X[:, m, :], x_in[:, m, :]).then_inc(x_in_s[m], 16)
            sp.dma_start(par[:, :], par_in).then_inc(par_s, 16)
            sp.dma_start(ident[:, :], consts[:, 0:P]).then_inc(const_s, 16)
            sp.dma_start(bones[:, :], consts[:, P:2 * P]).then_inc(const_s, 16)
            sp.dma_start(slopes[:, :], consts[:, C_SLOPES:C_SLOPES + NH + 1]).then_inc(const_s, 16)
            for name, _, _ in SEGMENTS:
                segment(name, {"gu0a": 0, "gu1a": 12}.get(name))
            for m in range(DC):
                sp.wait_ge(evac_s, SEGS["dn2b"].tile0 + m + 1)
                sp.dma_start(out[:, m, :], X[:, m, :]).then_inc(out_s, 16)
            sp.wait_ge(out_s, 16 * DC)


        @block.gpsimd
        def _(pool):
            nc.gpsimd.memset(ones[:, :], 1.0).then_inc(ones_s, 1)

            def segment(name):
                seg = SEGS[name]

                def body(i):
                    for k in range(seg.upb):
                        s, n = k % 2, seg.size
                        pool.wait_ge(hi_s, seg.unit0 + seg.upb * i + k + 1)
                        nc.gpsimd.tensor_tensor(WL[:, s, 0:n], WR[:, s, 0:n], WH[:, s, 0:n].bitcast(F32),
                                                ALU.subtract).then_inc(lo_s, 1)
                if name != "qkv":
                    loop(pool, 0, seg.bodies, [], body)
                    return

                def turn(r):
                    for b in range(3):
                        body(3 * r + b)

                    for k in range(32):
                        w = P * (k % 4) + P
                        pool.wait_ge(ss_c, 32 * r + k + 1)
                        nc.gpsimd.tensor_tensor(CC[:, k % 6, 0:w], XM[:, k % 3, 0:w], CC[:, k % 6, 0:w],
                                                ALU.subtract).then_inc(ss_w, 1)
                loop(pool, 0, 2, [], turn)

            for name, _, _ in SEGMENTS:
                segment(name)


        @block.tensor
        def _(pe):
            def dense(name, xh, xl, ready=None, after=None, only=None):
                seg = SEGS[name]

                def body(i, first=False):
                    for k in range(seg.upb):
                        s = k % 2
                        wh = WH[:, s, 0:seg.size].rearrange("p (c m) -> p c m", c=seg.chunks)
                        wl = WL[:, s, 0:seg.size].rearrange("p (c m) -> p c m", c=seg.chunks)
                        pe.wait_ge(lo_s, seg.unit0 + seg.upb * i + k + 1)
                        for m in range(seg.tiles):
                            b = k * seg.tiles + m
                            t = seg.tile0 + NB * i + b
                            if not isinstance(t, int) or t >= NB:
                                pe.wait_ge(evac_s, t - NB + 1)
                            cols = slice(m * P, m * P + P)
                            for c in range(seg.chunks):
                                if first and ready and b == 0:
                                    ready(c)
                                pe_h, pe_l = xh(c), xl(c)
                                nc.tensor.matmul(PS[:, b, :], wh[:, c, cols], pe_h, start=c == 0, stop=False)
                                nc.tensor.matmul(PS[:, b, :], wh[:, c, cols], pe_l, start=False, stop=False)
                                last = nc.tensor.matmul(PS[:, b, :], wl[:, c, cols], pe_h, start=False,
                                                        stop=c == seg.chunks - 1)
                            last.then_inc(tile_s, 1)
                            if after:
                                after(b)
                if only is not None:
                    body(only, ready is not None)
                    return
                body(0, True)
                loop(pe, 1, seg.bodies, [], body)

            def from_h(name, ready=None):
                dense(name, lambda c: Hh[:, c, :], lambda c: Hl[:, c, :], ready)

            def from_g(name, ready=None):
                dense(name, lambda c: Gh[:, c, :], lambda c: Gl[:, c, :], ready)

            norms = [0]

            def norm_stats():
                k = norms[0]
                norms[0] += 1
                pe.wait_ge(ss_s, (DC - 1) * (k + 1))
                nc.tensor.matmul(PS[:, 4, :], ones[:, :], ACC[:, :], start=True, stop=True).then_inc(mean_t, 1)

            def h_ready(c):
                pe.wait_ge(h_s, DC * hs[0] + c + 1)

            def g_ready(c):
                pe.wait_ge(g_s, gs[0] + c + 1)
            hs, gs = [0], [0]

            def feed_forward(l):
                norm_stats()
                for r, (half, n) in enumerate((("a", F1), ("b", F2))):
                    from_h(f"gu{l}{half}", h_ready if r == 0 else None)
                    if r == 0:
                        hs[0] += 1
                        if l < 2:
                            mod_sums(l)
                    from_g(f"dn{l}{half}", g_ready)
                    gs[0] += n

            def mod_sums(l):
                pe.wait_ge(ada_acc_s, 12 * (l + 1))
                if l:
                    pe.wait_ge(mod_done, 1)
                for n in range(24):
                    mm = nc.tensor.matmul(PS[:, 5, n:n + 1], AACC[:, n * P:n * P + P], ones[:, 0:1],
                                          start=True, stop=True)
                mm.then_inc(mod_sum, 1)

            pe.wait_ge(ones_s, 1)
            norm_stats()
            from_h("win", h_ready)
            hs[0] += 1
            from_g("wout", g_ready)
            gs[0] += DC
            feed_forward(0)
            def turn_values():
                end = SEGS["wkv"].tile0 + 12
                pe.wait_ge(evac_s, end)
                pe.wait_ge(const_s, 48)
                for n, (br, a) in enumerate(((0, 0), (0, 1), (1, 0), (1, 1))):
                    if n >= 2:
                        pe.wait_ge(vt_s, n - 1)
                    for kb in range(QB):
                        mm = nc.tensor.transpose(PS[:, 5 + n % 2, kb * P:kb * P + P],
                                                 KV[:, 6 + 4 * br + a, kb * P:kb * P + P], ident[:, :])
                    mm.then_inc(vt_t, 1)

            def narrow_products(bank, wh, wl, done):
                for c in range(DC):
                    nc.tensor.matmul(PS[:, bank, :], wh[:, c, :], Hh[:, c, :], start=c == 0, stop=False)
                    nc.tensor.matmul(PS[:, bank, :], wh[:, c, :], Hl[:, c, :], start=False, stop=False)
                    mm = nc.tensor.matmul(PS[:, bank, :], wl[:, c, :], Hh[:, c, :], start=False, stop=c == DC - 1)
                mm.then_inc(done, 1)

            def turn_rows(bank, rows, n, done):
                for qb in range(QB):
                    mm = nc.tensor.transpose(PS[:, bank, qb * n:qb * n + n], rows[0:n, qb * P:qb * P + P],
                                             ident[0:n, 0:n])
                mm.then_inc(done, 1)

            def hidden_rows(s, j0):
                if j0 == 0:
                    pe.wait_ge(w1_s[s], 16)
                pe.wait_ge(xj_s, 4 * s + j0 // 4 + 1)
                for j in range(j0, j0 + 4):
                    for mc in range(2):
                        mm = nc.tensor.matmul(PS[:, 4 + 2 * s + mc, 0:4 * CG], W1[s][:, j, mc * P:mc * P + P],
                                              XJ[:, s, j, :, :].rearrange("p g n -> p (g n)"),
                                              start=j == 0, stop=j == 15)
                mm.then_inc(xj_used, 1)

            def compress():
                for s in range(2):
                    pe.wait_ge(hid_s, 2 * s + 2)
                    if s == 0:
                        w2 = pcol("w2k", 0, 256).rearrange("p (c m) -> p c m", c=2)
                        for mc in range(2):
                            mm = nc.tensor.matmul(PS[:, 5, 0:4 * CG], w2[:, mc, :],
                                                  HID[:, mc, :, :].rearrange("p g n -> p (g n)"),
                                                  start=mc == 0, stop=mc == 1)
                    else:
                        w2 = pcol("w2v", 0, 128).rearrange("p (c m) -> p c m", c=2)
                        for g in range(4):
                            for mc in range(2):
                                rows = HIDR[:, mc, g, :, :].rearrange("p r n -> p (r n)")
                                mm = nc.tensor.matmul(PS[:, 6, g * HD:(g + 1) * HD], rows, w2[:, mc, :],
                                                      start=mc == 0, stop=mc == 1)
                    mm.then_inc(kvc_t, 1)

            def compressed_attention():
                pe.wait_ge(kvc_s, 3)
                pe.wait_ge(gt_s, 1)
                pe.wait_ge(evac_s, SEGS["wq"].tile0 + DC)
                for k in range(QB + 1):
                    if k < QB:
                        if k >= 2:
                            pe.wait_ge(sc_m, k - 1)
                        for pair in range(DC):
                            a, j = pair // 4, pair % 4
                            o = PS[:, 4 + k % 2, 2 * P * a:2 * P * a + 2 * P].rearrange("p (b x) -> p b x", b=2)
                            mm = nc.tensor.matmul(o[:, :, j * CG:j * CG + CG], QT[:, pair, k * P:k * P + P],
                                                  KC[:, a, :, :], start=True, stop=True)
                        mm.then_inc(sc_t, 1)
                    if k:
                        qb = k - 1
                        pe.wait_ge(sc_n, qb + 1)
                        if qb:
                            pe.wait_ge(pc_s, qb)
                        for g in range(4):
                            mm = nc.tensor.transpose(PS[:, 6, g * P:g * P + P],
                                                     SE[:, qb % 2, g * P:g * P + P], ident[:, :])
                        mm.then_inc(pc_t, 1)
                pe.wait_ge(pc_s, QB)
                for pair in range(DC):
                    b = pair % 4
                    if pair >= 4:
                        pe.wait_ge(oc_s, pair - 3)
                    j = pair % 4
                    for hf in range(2):
                        g = 2 * (pair // 4) + hf
                        mm = nc.tensor.matmul(PS[HD * hf:HD * hf + HD, b, :], VC[CG * j:CG * j + CG, g, :],
                                              PCT[CG * j:CG * j + CG, g, :], start=True, stop=True)
                    mm.then_inc(oc_t, 1)

            def attention():
                pe.wait_ge(oc_s, DC)

                def turn(first, base, kv_tile):
                    def step_of(k):
                        return k // 16, k // 8 % 2, k // 4 % 2, k % 4

                    for k in range(32 + 7):
                        if k < 32:
                            pp, hf, br, qb = step_of(k)
                            half = slice(HD * hf, HD * hf + HD)
                            if k % 16 == 0:
                                pe.wait_ge(stage_s, base(2) + pp + 1)
                            if k >= 4:
                                pe.wait_ge(s_m, base(32) + k - 3)
                            elif not first:
                                pe.wait_ge(s_m, base(32))
                            nc.tensor.matmul(PS[:, (4, 5, 6, 2)[k % 4], 0:P * qb + P], QS[half, pp, qb * P:qb * P + P],
                                             kv_tile(half, 4 + 4 * br, P * qb + P), start=True, stop=True)\
                                .then_inc(s_t, 1)
                        if 6 <= k < 38:
                            m = k - 6
                            pp, hf, br, qb = step_of(m)
                            pe.wait_ge(s_n, base(32) + m + 1)
                            if m >= 2 or not first:
                                pe.wait_ge(p_s, base(32) + max(m - 1, 0))
                            for kb in range(qb + 1):
                                mm = nc.tensor.transpose(PS[:, (7, 3)[m % 2], kb * P:kb * P + P],
                                                         PB[:, m % 6, kb * P:kb * P + P], ident[:, :])
                            mm.then_inc(p_t, 1)
                        if k >= 7 and (k - 7) % 4 == 3:
                            pp, hf, br, _ = step_of(k - 7)
                            n = (k - 7) // 4
                            pe.wait_ge(p_s, base(32) + k - 6)
                            if n % 4 == 0 and not first:
                                pe.wait_ge(o_s, base(2) + pp - 1)
                            for kb in range(QB):
                                mm = nc.tensor.matmul(PS[HD * hf:HD * hf + HD, pp, kb * P:T],
                                                      VT[:, br, kb, kt * P + HD * hf:kt * P + HD * hf + HD],
                                                      PT[:, n % 2, kb, kb * P:T], start=br == 0 and kb == 0,
                                                      stop=br == 1 and kb == QB - 1)
                            mm.then_inc(o_t, 1)

                for kt in range(2):
                    def keys(half, tile, n):
                        return KV[half, tile + kt, 0:n]
                    if kt == 0:
                        turn(True, lambda k: 0, keys)
                        loop(pe, 1, 2, [], lambda i: turn(False, lambda k: k, keys))
                    else:
                        loop(pe, 2, 4, [], lambda i: turn(False, lambda k: k * i, keys))

            norm_stats()
            from_h("wkv", h_ready)
            hs[0] += 1
            turn_values()
            def hidden_after(i):
                return lambda b: hidden_rows(i, 4 * b)
            dense("wq", lambda c: Hh[:, c, :], lambda c: Hl[:, c, :], h_ready, after=hidden_after(0), only=0)
            dense("wq", lambda c: Hh[:, c, :], lambda c: Hl[:, c, :], after=hidden_after(1), only=1)
            hs[0] += 1
            pe.wait_ge(gw_s, 1)
            pe.wait_ge(hid_s, 2)
            narrow_products(4, GWH, GWL, gt_r)
            compress()
            pe.wait_ge(go_s, 1)
            turn_rows(4, GO, 3 * NH, gt_t)
            compressed_attention()
            attention()
            dense("wo", lambda c: Hh[:, c, :], lambda c: Hl[:, c, :], lambda c: pe.wait_ge(o_s, DC))
            feed_forward(1)
            def stick_breaking(r):
                def bones_product(n):
                    pe.wait_ge(sq2_s, 8 * r + n + 1)
                    nc.tensor.matmul(PS[:, 4 + n % 2, :], bones[:, :], SQ2[:, n % 2, :], start=True, stop=True)\
                        .then_inc(n2_t, 1)

                tile0 = SEGS["qkv"].tile0
                for b3 in range(3):
                    def after(b):
                        n = 4 * b3 + b
                        if 1 <= n <= 8:
                            bones_product(n - 1)
                    dense("qkv", lambda c: Hh[:, c, :], lambda c: Hl[:, c, :], after=after, only=3 * r + b3)
                for a in range(4):
                    pe.wait_ge(evac_s, tile0 + 12 * r + 9 + a)
                    if a >= 2:
                        pe.wait_ge(vs_e, 4 * r + a - 1)
                    for kb in range(QB):
                        mm = nc.tensor.transpose(PS[:, 6 + a % 2, kb * P:kb * P + P],
                                                 QKV[:, 8 + a, kb * P:kb * P + P], ident[:, :])
                    mm.then_inc(vs_t, 1)
                pe.wait_ge(qk_s, 8 * r + 8)
                pe.wait_ge(vs_e, 4 * r + 4)
                for k in range(32 + 8):
                    if k < 32:
                        a, hf, qb = k // 8, k // 4 % 2, k % 4
                        half = slice(HD * hf, HD * hf + HD)
                        if k >= 4:
                            pe.wait_ge(ss_x, 32 * r + k - 3)
                        nc.tensor.matmul(PS[:, 4 + k % 4, 0:P * qb + P], QKV[half, a, qb * P:qb * P + P],
                                         QKV[half, 4 + a, 0:P * qb + P], start=True, stop=True).then_inc(ss_t, 1)
                    if 7 <= k < 39:
                        m = k - 7
                        pe.wait_ge(ss_e, 32 * r + m + 1)
                        if m >= 2:
                            pe.wait_ge(st_s, 32 * r + m - 1)
                        for kb in range(m % 4 + 1):
                            mm = nc.tensor.transpose(PS[:, m % 2, kb * P:kb * P + P],
                                                     CC[:, m % 6, kb * P:kb * P + P], ident[:, :])
                        mm.then_inc(st_t, 1)
                    if k >= 8 and (k - 8) % 4 == 3:
                        h = (k - 8) // 4
                        a, hf = h // 2, h % 2
                        pe.wait_ge(st_s, 32 * r + 4 * h + 4)
                        if a >= 2 and hf == 0:
                            pe.wait_ge(so_s, 4 * r + a - 1)
                        for kb in range(QB):
                            mm = nc.tensor.matmul(PS[HD * hf:HD * hf + HD, 2 + a % 2, kb * P:T],
                                                  VTS[:, kb, a * P + HD * hf:a * P + HD * hf + HD],
                                                  PTS[h % 2][:, kb, kb * P:T], start=kb == 0, stop=kb == QB - 1)
                        mm.then_inc(so_t, 1)
                pe.wait_ge(so_s, 4 * r + 4)

            def attention_part(m):
                seg = SEGS["wog"]
                s, k = m // seg.tiles % 2, m % seg.tiles
                if k == 0:
                    pe.wait_ge(lo_s, seg.unit0 + m // seg.tiles + 1)
                pe.wait_ge(evac_s, seg.tile0 + m)
                wh = WH[:, s, :].rearrange("p (c m) -> p c m", c=DC)[:, :, k * P:k * P + P]
                wl = WL[:, s, :].rearrange("p (c m) -> p c m", c=DC)[:, :, k * P:k * P + P]
                for c in range(DC):
                    nc.tensor.matmul(PS[:, 7, :], wh[:, c, :], Gh[:, c, :], start=c == 0, stop=False)
                    nc.tensor.matmul(PS[:, 7, :], wh[:, c, :], Gl[:, c, :], start=False, stop=False)
                    mm = nc.tensor.matmul(PS[:, 7, :], wl[:, c, :], Gh[:, c, :], start=False, stop=c == DC - 1)
                mm.then_inc(tile_s, 1)

            def ssd_chunk(c):
                pe.wait_ge(ch_s, c + 1)
                pe.wait_ge(ncs_s, 1)
                pe.wait_ge(ac_s, c + 1)
                for f in range(DC):
                    nc.tensor.transpose(PS[:, 2 + f // 4, (f % 4) * P:(f % 4) * P + P], CH[:, f, :], ident[:, :])
                for g in range(2):
                    nc.tensor.transpose(PS[:, 4, (2 + g) * P:(3 + g) * P], CH[:, 8 + g, :], ident[:, :])
                for g in range(2):
                    mm = nc.tensor.matmul(PS[:, 4, g * P:g * P + P], CH[:, 8 + g, :], CH[:, 10 + g, :],
                                          start=True, stop=True)
                mm.then_inc(xt_t, 1)
                for q in range(2):
                    if q:
                        pe.wait_ge(lm_s, 2 * c + 1)
                    for h in range(8):
                        w = ADTC[:, 8 * q + h:8 * q + h + 1].to_broadcast([P, P])
                        mm = nc.tensor.matmul(PS[:, h // 4, (h % 4) * P:(h % 4) * P + P], w, TRI,
                                              start=True, stop=True)
                    mm.then_inc(cb_t, 1)
                for g in range(2):
                    nc.tensor.matmul(PS[:, 5 + g, :], CH[:, 10 + g, :],
                                     PREV[:, 8 * g:8 * g + 8, :].rearrange("p h d -> p (h d)"), start=True, stop=True)
                attention_part(2 * c)
                for q in range(2):
                    pe.wait_ge(mm_s, 2 * c + q + 1)
                    for h in range(8 * q, 8 * q + 8):
                        nc.tensor.matmul(PS[:, 2 + q, (h % 8) * HD:(h % 8) * HD + HD], LM[:, h, :], XDT[:, h, :],
                                         start=True, stop=True)
                pe.wait_ge(xdt_s, c + 1)
                for g in range(2):
                    mm = nc.tensor.matmul(PS[:, g, :], BTK[:, g, :],
                                          XDD[:, 8 * g:8 * g + 8, :].rearrange("p h d -> p (h d)"),
                                          start=True, stop=True)
                mm.then_inc(yd_t, 1)
                attention_part(2 * c + 1)
                pe.wait_ge(y_s, c + 1)
                for f in range(DC):
                    mm = nc.tensor.transpose(PS[:, 5 + f // 4, (f % 4) * P:(f % 4) * P + P],
                                             YC[:, 2 * f:2 * f + 2, :].rearrange("p h d -> p (h d)"), ident[:, :])
                mm.then_inc(yt_t, 1)

            def z_products():
                def sum_product(m):
                    pe.wait_ge(sq3_s, m + 1)
                    nc.tensor.matmul(PS[:, 5 + m // 4, :], ones[:, :], SQ3[:, m % 2, :], start=m % 4 == 0,
                                     stop=m % 4 == 3).then_inc(z_t, 1)
                for i in range(2):
                    def after(b):
                        if 4 * i + b:
                            sum_product(4 * i + b - 1)
                    dense("zg", lambda c: Hh[:, c, :], lambda c: Hl[:, c, :], after=after, only=i)
                sum_product(7)

            norm_stats()
            norm_stats()
            for c in range(DC):
                h_ready(c)
            hs[0] += 1
            loop(pe, 0, 2, [], stick_breaking)
            pe.wait_ge(dw_s, 1)
            narrow_products(7, DWH, DWL, dt_r)
            dense("xbc", lambda c: Hh[:, c, :], lambda c: Hl[:, c, :], only=0)
            pe.wait_ge(dr_s, 1)
            turn_rows(7, DTR, NH, dt_t)
            for i in range(1, 3):
                dense("xbc", lambda c: Hh[:, c, :], lambda c: Hl[:, c, :], only=i)
            pe.wait_ge(dt_s, 1)
            nc.tensor.matmul(PS[:, 6, 0:QB * NH], TRI, ADT[:, :, :].rearrange("p q h -> p (q h)"),
                             start=True, stop=True).then_inc(cs_t, 1)
            for c in range(QB):
                ssd_chunk(c)
            pe.wait_ge(ck_s, QB)
            z_products()
            from_h("woh", lambda c: pe.wait_ge(yo_s, c + 1))
            norm_stats()
            from_h("gu2a", h_ready)
            from_g("dn2a", g_ready)
            gs[0] += F1
            from_h("gu2b")
            from_g("dn2b", g_ready)




        @block.scalar
        def _(act):
            chain = Tally(act, a_chain)
            norms = [0]

            def hi(u, i=None, per=0, size=0):
                if u >= UNITS:
                    return
                s = u % 2
                if i is None:
                    n = UNIT_SIZE[u]
                    act.wait_ge(raw_s[s], 16 * (u // 2 + 1))
                    if u >= 2:
                        act.wait_ge(tile_s, TILES_AFTER[u - 2])
                else:
                    n = size
                    act.wait_ge(raw_s[s], 16 * (u // 2 + 1) + 8 * per * i)
                    act.wait_ge(tile_s, TILES_AFTER[u - 2] + NB * i)
                nc.scalar.activation(WH[:, s, 0:n], WR[:, s, 0:n], ACT.Copy).then_inc(hi_s, 1)

            def dense(name, evac=None, per_turn=(), after_first=None):
                seg = SEGS[name]

                def body(i):
                    dynamic = not isinstance(i, int)
                    for k in range(seg.upb):
                        if evac:
                            evac(i, k)
                        if dynamic:
                            hi(seg.unit0 + k + 2, i, seg.upb, seg.size)
                        else:
                            hi(seg.unit0 + seg.upb * i + k + 2)
                if after_first:
                    body(0)
                    after_first()
                loop(act, 1 if after_first else 0, seg.bodies - 1, list(per_turn), body)
                body(seg.bodies - 1)

            def square(m):
                if m >= 3:
                    act.wait_ge(ss_s, (DC - 1) * norms[0] + m - 2)
                nc.scalar.activation(ACC[:, :] if m == 0 else SQ[:, m % 2, :], X[:, m, :], ACT.Square)\
                    .then_inc(sq_s, 1)

            def dense_squares(name):
                seg = SEGS[name]
                act.preload_act_table_set("natural_log_exp_and_others")
                for u in range(seg.units):
                    if u < seg.units - 1:
                        hi(seg.unit0 + u + 2)
                    for m in range(seg.tiles * u, seg.tiles * (u + 1)):
                        act.wait_ge(evac_s, seg.tile0 + m + 1)
                        square(m)
                    if u == seg.units - 1:
                        hi(seg.unit0 + u + 2)

            def norm_root(eps):
                k = norms[0]
                norms[0] += 1
                act.wait_ge(mean_t, k + 1)
                inverse_root(RS[:, :], PS[:, 4, :], 1.0 / D, eps).then_inc(rt_s, 1)

            def inverse_root(dst, src, scale, eps):
                chain.mark(nc.scalar.activation(dst, src, ACT.Ln, scale=scale, bias=eps_col(eps)))
                chain.wait()
                return nc.scalar.activation(dst, dst, ACT.Exp, scale=-0.5)

            def norm_hi(shift=None):
                hs = hi_n[0]
                hi_n[0] += DC
                for m in range(DC):
                    act.wait_ge(xn_s, hs + m + 1)
                    if shift is None:
                        ins = nc.scalar.activation(Hh[:, m, :], XN[:, m % 3, :], ACT.Copy)
                    else:
                        ins = nc.scalar.activation(Hh[:, m, :], XN[:, m % 3, :], ACT.Identity, bias=shift(m))
                    ins.then_inc(hh_s, 1)
            hi_n = [0]

            def eps_col(eps):
                return EPSC[:, 0:1] if eps == EPS1 else EPSC[:, 1:2]

            def feed_forward(l, eps, shift=None):
                norm_root(eps)
                norm_hi(shift)
                for half, n in (("a", F1), ("b", F2)):
                    seg = SEGS[f"gu{l}{half}"]

                    def evac(i, k):
                        t = seg.tile0 + NB * i + 2 * k
                        act.wait_ge(tile_s, t + 1)
                        act.wait_ge(evac_s, t - 2)
                        nc.scalar.activation(SG[:, k, :], PS[:, 2 * k, :], ACT.Silu).then_inc(sg_s, 1)
                    dense(f"gu{l}{half}", evac)
                    if half == "b" and l < 2:
                        dense_squares(f"dn{l}{half}")
                    else:
                        dense(f"dn{l}{half}")

            def conv_evac():
                seg = SEGS["win"]
                for u in range(seg.units):
                    for t in (2 * u, 2 * u + 1):
                        if t % 3 == 0:
                            j = t // 3
                            act.wait_ge(tile_s, t + 1)
                            if j >= 2:
                                act.wait_ge(evac_s, 3 * (j - 2) + 2)
                            nc.scalar.activation(CT[:, j % 2, :], PS[:, t % NB, :], ACT.Copy).then_inc(ct_s, 1)
                    hi(u + 2)

            act.preload_act_table_set("natural_log_exp_and_others")
            for m in range(DC):
                act.wait_ge(x_in_s[m], 16)
                square(m)
            hi(0)
            hi(1)
            act.wait_ge(eps_s, 2)
            norm_root(EPS1)
            norm_hi()
            act.wait_ge(par_s, 16)
            nc.scalar.activation(CSIL[:, :], pcol("cond", 0, 8), ACT.Silu).then_inc(cs_s, 1)
            conv_evac()
            dense_squares("wout")
            feed_forward(0, EPS1)
            def load_compression():
                act.wait_ge(evac_s, SEGS["wkv"].tile0 + 12)
                for s in range(2):
                    for g in range(4):
                        src = KV[HD * (g % 2):HD * (g % 2) + HD, 2 * s + g // 2, :]
                        act.dma_start(RW[s][0:HD, g, :], src).then_inc(rw_s[s], 16)
                        act.dma_start(RW[s][HD:P, g, 0:T - 1], src[:, 1:T]).then_inc(rw_s[s], 16)
                    act.dma_start(W1[s][:, :, :], (w1k, w1v)[s].rearrange("p (j m) -> p j m", j=16))\
                        .then_inc(w1_s[s], 16)

            def hidden_out():
                for s in range(2):
                    for mc in range(2):
                        act.wait_ge(xj_used, 4 * s + 4)
                        src = PS[:, 4 + 2 * s + mc, 0:4 * CG].rearrange("p (g n) -> p g n", g=4)
                        if s == 0:
                            nc.scalar.activation(HID[:, mc, :, :], src, ACT.Silu).then_inc(hid_s, 1)
                        else:
                            nc.scalar.activation(HIDR[:, mc, :, :, :],
                                                 src.unsqueeze(2).to_broadcast([P, 4, 4, CG]), ACT.Silu)\
                                .then_inc(hid_s, 1)

            def compress():
                act.wait_ge(kvc_t, 1)
                keys = PS[:, 5, 0:4 * CG].rearrange("p (a b n) -> p a b n", a=2, b=2)
                for b in range(2):
                    half = slice(HD * b, HD * b + HD)
                    nc.scalar.activation(KC[half, :, b, :], keys[half, :, b, :], ACT.Copy).then_inc(kvc_s, 1)
                act.wait_ge(kvc_t, 2)
                nc.scalar.activation(VC[:, :, :].rearrange("p g d -> p (g d)"), PS[:, 6, 0:4 * HD],
                                     ACT.Copy).then_inc(kvc_s, 1)

            def load_distances():
                act.wait_ge(rw_s[0], 128)
                act.wait_ge(rw_s[1], 128)
                act.dma_start(DIST[:, :], consts[:, C_DIST:C_DIST + T]).then_inc(dist_s, 16)
                act.dma_start(DISTC[:, :, :], consts[:, C_DISTC:C_DISTC + QB * CG].rearrange(
                    "p (a n) -> p a n", a=QB)).then_inc(dist_s, 16)

            def compressed_attention():
                for k in range(QB + 1):
                    if k < QB:
                        act.wait_ge(sc_m, k + 1)
                        if k >= 2:
                            act.wait_ge(pc_t, k - 1)
                        nc.scalar.activation(SE[:, k % 2, :], SC[:, k % 2, :], ACT.Exp).then_inc(sc_e, 1)
                    if k:
                        qb = k - 1
                        act.wait_ge(pc_t, qb + 1)
                        nc.scalar.activation(PCT[:, :, qb * P:qb * P + P],
                                             PS[:, 6, :].rearrange("p (g q) -> p g q", g=4), ACT.Copy)\
                            .then_inc(pc_s, 1)
                for pair in range(DC):
                    act.wait_ge(oc_t, pair + 1)
                    nc.scalar.activation(OC[:, pair, :], PS[:, pair % 4, :], ACT.Copy).then_inc(oc_s, 1)

            def attention():
                act.wait_ge(dist_s, 32)

                def turn(first, i, base):
                    def stage(pp):
                        if not first:
                            act.wait_ge(s_t, base(32))
                            act.wait_ge(s_m, base(32))
                        nc.scalar.activation(QS[:, pp, :], QT[:, DS(2 * i + pp, 1), :].rearrange("p a t -> p (a t)"),
                                             ACT.Copy).then_inc(stage_s, 1)
                        for hf in range(2):
                            h = 8 * kt + 4 * hf + 2 * (i - 2 * kt) + pp
                            nc.scalar.activation(BIAS[:, 2 * pp + hf, :], DIST[:, :], ACT.Copy,
                                                 scale=slopes[:, DS(h, 1)]).then_inc(bias_s, 1)

                    stage(0)
                    for k in range(32 + 4):
                        if k == 8:
                            stage(1)
                        if k < 32:
                            act.wait_ge(s_m, base(32) + k + 1)
                            w = P * (k % 4) + P
                            nc.scalar.activation(PB[:, k % 6, 0:w], PB[:, k % 6, 0:w], ACT.Exp,
                                                 bias=NMX[:, 1, k:k + 1], accum_out=SMX[:, 0, k:k + 1])\
                                .then_inc(s_e, 1)
                        if k >= 4:
                            m = k - 4
                            qb, n = m % 4, m // 4
                            act.wait_ge(p_t, base(32) + m + 1)
                            if n >= 2 or not first:
                                act.wait_ge(o_t, base(8) + n - 1)
                            nc.scalar.activation(PT[:, n % 2, 0:qb + 1, qb * P:qb * P + P],
                                                 PS[:, (7, 3)[m % 2], 0:P * qb + P].rearrange("p (k q) -> p k q", q=P),
                                                 ACT.Copy).then_inc(p_s, 1)

                for kt in range(2):
                    if kt == 0:
                        turn(True, 0, lambda k: 0)
                        loop(act, 1, 2, [], lambda i: turn(False, i, lambda k: k * i))
                    else:
                        loop(act, 2, 4, [], lambda i: turn(False, i, lambda k: k * i))

            norm_root(EPS1)
            norm_hi()
            dense("wkv")
            load_compression()
            for n, (br, a) in enumerate(((0, 0), (0, 1), (1, 0), (1, 1))):
                act.wait_ge(vt_t, n + 1)
                nc.scalar.activation(VT[:, br, :, a * P:a * P + P],
                                     PS[:, 5 + n % 2, :].rearrange("p (k d) -> p k d", d=P), ACT.Copy)\
                    .then_inc(vt_s, 1)
            norm_hi()
            load_distances()
            dense("wq")
            hidden_out()
            act.wait_ge(gt_r, 1)
            nc.scalar.activation(GO[0:3 * NH, :], PS[0:3 * NH, 4, :], ACT.Sigmoid).then_inc(go_s, 1)
            compress()
            act.wait_ge(gt_t, 1)
            nc.scalar.activation(GT[:, :, :].rearrange("p q h -> p (q h)"), PS[:, 4, 0:3 * NH * QB], ACT.Copy)\
                .then_inc(gt_s, 1)
            compressed_attention()
            attention()
            dense_squares("wo")
            feed_forward(1, EPS1)
            def stick_breaking(r):
                act.preload_act_table_set("natural_log_exp_and_others")
                seg = SEGS["qkv"]

                def square_rows(n):
                    act.wait_ge(evac_s, seg.tile0 + 12 * r + n + 1)
                    nc.scalar.activation(SQ2[:, n % 2, :], QKV[:, n, :], ACT.Square).then_inc(sq2_s, 1)

                def root(n):
                    act.wait_ge(n2_t, 8 * r + n + 1)
                    if n >= 2:
                        act.wait_ge(qk_s, 8 * r + n - 1)
                    inverse_root(RT2[:, n % 2, :], PS[:, 4 + n % 2, :], 1.0 / HD, EPS2).then_inc(r2_s, 1)
                for u in range(6):
                    for n in (2 * u, 2 * u + 1):
                        if n < 8:
                            square_rows(n)
                        if n % 2 == 0 and 1 <= n <= 8:
                            root(n - 1)
                    if isinstance(r, int):
                        hi(seg.unit0 + 6 * r + u + 2)
                    else:
                        hi(seg.unit0 + u % 2 + 2, 3 * r + u // 2, seg.upb, seg.size)
                    if u < 4:
                        root(2 * u)
                for a in range(4):
                    act.wait_ge(vs_t, 4 * r + a + 1)
                    nc.scalar.activation(VTS[:, :, a * P:a * P + P],
                                         PS[:, 6 + a % 2, :].rearrange("p (k d) -> p k d", d=P), ACT.Copy)\
                        .then_inc(vs_e, 1)
                for k in range(32 + 5):
                    if k < 32:
                        w = P * (k % 4) + P
                        act.wait_ge(ss_x, 32 * r + k + 1)
                        chain.mark(nc.scalar.activation(EE[:, k % 2, 0:w], EE[:, k % 2, 0:w], ACT.Exp))
                    if 3 <= k < 35:
                        m = k - 3
                        wm = P * (m % 4) + P
                        act.wait_ge(ss_w, 32 * r + m + 1)
                        nc.scalar.activation(CC[:, m % 6, 0:wm], CC[:, m % 6, 0:wm], ACT.Exp).then_inc(ss_e, 1)
                    if k < 32:
                        chain.wait()
                        nc.scalar.activation(EE[:, k % 2, 0:w], EE[:, k % 2, 0:w], ACT.Ln, bias=1.0)\
                            .then_inc(ss_l, 1)
                    if k >= 5:
                        m = k - 5
                        qb, h = m % 4, m // 4
                        act.wait_ge(st_t, 32 * r + m + 1)
                        if h >= 2:
                            act.wait_ge(so_t, 8 * r + h - 1)
                        nc.scalar.activation(PTS[h % 2][:, 0:qb + 1, qb * P:qb * P + P],
                                             PS[:, m % 2, 0:P * qb + P].rearrange("p (k q) -> p k q", q=P),
                                             ACT.Copy).then_inc(st_s, 1)

            def dt_log():
                act.preload_act_table_set("natural_log_exp_and_others")
                act.wait_ge(dt_a, 2)
                flat = DTE[:, :, :].rearrange("p q h -> p (q h)")
                chain.mark(nc.scalar.activation(flat, flat, ACT.Exp))
                chain.wait()
                nc.scalar.activation(flat, flat, ACT.Ln, bias=1.0).then_inc(dt_e, 1)
                nc.scalar.activation(AN[:, :], pcol("alog", 0, NH), ACT.Exp).then_inc(dt_e, 1)

            def ssd_chunk(c):
                if c:
                    act.wait_ge(ck_s, c)
                else:
                    act.wait_ge(xb_s, 12)
                nc.scalar.activation(CH[:, :, :], XB[:, :, DS(P * c, P)], ACT.Copy).then_inc(ch_s, 1)
                for q in range(2):
                    act.wait_ge(lm_s, 2 * c + q + 1)
                    for h in range(8 * q, 8 * q + 8):
                        ins = nc.scalar.activation(LM[:, h, :], LM[:, h, :], ACT.Exp,
                                                   bias=NCS[:, DS(c, 1), h:h + 1].rearrange("p a h -> p (a h)"))
                    ins.then_inc(le_s, 1)
                act.wait_ge(ex_s, c + 1)
                nc.scalar.activation(EX[:, :, :], EX[:, :, :], ACT.Exp).then_inc(de_s, 1)
                hi(SEGS["wog"].unit0 + c + 2)

            def z_evac():
                seg = SEGS["zg"]

                def root(g):
                    act.wait_ge(z_t, 4 * g + 4)
                    inverse_root(RZ[:, g, :], PS[:, 5 + g, :], 2.0 / D, EPS2).then_inc(rz_s, 1)
                for u in range(4):
                    for m in (2 * u, 2 * u + 1):
                        act.wait_ge(tile_s, seg.tile0 + m + 1)
                        if m >= 2:
                            act.wait_ge(evac_s, seg.tile0 + m - 1)
                        nc.scalar.activation(SZ[:, m % 2, :], PS[:, m % NB, :], ACT.Silu).then_inc(sz_s, 1)
                        act.wait_ge(evac_s, seg.tile0 + m + 1)
                        if m >= 2:
                            act.wait_ge(z_t, m - 1)
                        nc.scalar.activation(SQ3[:, m % 2, :], XB[:, m, :], ACT.Square).then_inc(sq3_s, 1)
                    hi(seg.unit0 + u + 2)
                for g in range(2):
                    root(g)

            act.wait_ge(gw_s, 1)
            act.wait_ge(o_s, DC)
            act.dma_start(par[:, COL["gatew"]:COL["gatew"] + 3 * P], consts[:, C_TRI:C_TRI + 3 * P])\
                .then_inc(mask_s, 16)
            norm_root(EPS1)
            for m in range(DC):
                act.wait_ge(xf_s, m + 1)
                square(m)
            norm_root(EPS2)
            norm_hi(lambda m: MOD[:, m:m + 1])
            loop(act, 0, 2, [(chain, 32 + 8)], stick_breaking)

            def silu_xbc(i, k):
                for m in range(2):
                    t = 4 * i + 2 * k + m
                    act.wait_ge(ca_s, t + 1)
                    nc.scalar.activation(XB[:, DS(t, 1), :].rearrange("p a t -> p (a t)"), CA[:, m, :], ACT.Silu)\
                        .then_inc(xb_s, 1)
            act.wait_ge(dt_r, 1)
            nc.scalar.activation(DTR[0:NH, :], PS[0:NH, 7, :], ACT.Copy).then_inc(dr_s, 1)
            dense("xbc", silu_xbc, after_first=dt_log)
            for c in range(QB):
                ssd_chunk(c)
            z_evac()
            dense_squares("woh")
            feed_forward(2, EPS2, lambda m: MOD[:, 24 + m:25 + m])




        @block.vector
        def _(dve):
            chain = Tally(dve, v_chain)
            norms, sgs = [0], [0]

            def row(tensor, m):
                return tensor[:, DS(m, 1), :].rearrange("p a t -> p (a t)")

            def split(dst_h, dst_l, src, sem_):
                chain.mark(nc.vector.tensor_copy(dst_h, src))
                chain.wait()
                nc.vector.tensor_tensor(dst_l, src, dst_h.bitcast(F32), ALU.subtract).then_inc(sem_, 1)

            def add_squares(m):
                k = norms[0]
                if m == 0:
                    return
                dve.wait_ge(sq_s, DC * k + m + 1)
                if m >= 2:
                    dve.wait_ge(ss_s, (DC - 1) * k + m - 1)
                nc.vector.tensor_tensor(ACC[:, :], ACC[:, :], SQ[:, m % 2, :], ALU.add).then_inc(ss_s, 1)

            def norm(gain, shift=None, to_x=None, again=None):
                if again:
                    dve.wait_ge(tile_s, again)
                else:
                    norms[0] += 1
                    dve.wait_ge(rt_s, norms[0])
                if to_x:
                    for m in range(DC):
                        nc.vector.scalar_tensor_tensor(X[:, m, :], X[:, m, :], gain(m), RS[:, :], ALU.mult,
                                                       ALU.mult).then_inc(to_x, 1)
                        if m:
                            add_squares(m - 1)
                    add_squares(DC - 1)
                    return
                hs = h_count[0]
                for m in range(DC + 1):
                    if m < DC:
                        if m >= 3:
                            dve.wait_ge(h_s, hs + m - 2)
                        nc.vector.scalar_tensor_tensor(XN[:, m % 3, :], X[:, m, :], gain(m), RS[:, :],
                                                       ALU.mult, ALU.mult).then_inc(xn_s, 1)
                    if m:
                        n = m - 1
                        dve.wait_ge(hh_s, hs + m)
                        if shift:
                            ins = nc.vector.scalar_tensor_tensor(Hl[:, n, :], XN[:, n % 3, :], shift(n),
                                                                 Hh[:, n, :].bitcast(F32), ALU.add, ALU.subtract)
                        else:
                            ins = nc.vector.tensor_tensor(Hl[:, n, :], XN[:, n % 3, :],
                                                          Hh[:, n, :].bitcast(F32), ALU.subtract)
                        ins.then_inc(h_s, 1)
                h_count[0] += DC

            h_count, g_count = [0], [0]

            def conv_mixer():
                for j in range(DC):
                    t = 3 * j
                    dve.wait_ge(ct_s, j + 1)
                    dve.wait_ge(tile_s, t + 2)
                    nc.vector.tensor_tensor(CV[:, 2:T + 2], CT[:, j % 2, :], PS[:, (t + 1) % NB, :],
                                            ALU.mult).then_inc(evac_s, 2)
                    dve.wait_ge(evac_s, t + 2)
                    for tap in range(3):
                        w = pcol("conv1", 8 * tap + j)
                        if tap == 0:
                            chain.mark(nc.vector.tensor_scalar(CU[:, :], CV[:, 0:T], w, None, ALU.mult))
                        else:
                            chain.mark(nc.vector.scalar_tensor_tensor(CU[:, :], CV[:, tap:T + tap], w, CU[:, :],
                                                                      ALU.mult, ALU.add))
                        chain.wait()
                    dve.wait_ge(tile_s, t + 3)
                    if j:
                        dve.wait_ge(g_s, j)
                    nc.vector.tensor_tensor(HT[:, :], CU[:, :], PS[:, (t + 2) % NB, :], ALU.mult)\
                        .then_inc(evac_s, 1)
                    dve.wait_ge(evac_s, t + 3)
                    split(Gh[:, j, :], Gl[:, j, :], HT[:, :], g_s)
                g_count[0] += DC

            def residual(name, scale=None, squares=True):
                seg = SEGS[name]
                for m in range(DC):
                    dve.wait_ge(tile_s, seg.tile0 + m + 1)
                    if scale is None:
                        ins = nc.vector.tensor_tensor(X[:, m, :], X[:, m, :], PS[:, m % NB, :], ALU.add)
                    else:
                        ins = nc.vector.scalar_tensor_tensor(X[:, m, :], PS[:, m % NB, :], scale(m), X[:, m, :],
                                                             ALU.mult, ALU.add)
                    ins.then_inc(evac_s, 1)
                    if squares and m:
                        add_squares(m - 1)
                if squares:
                    add_squares(DC - 1)

            def feed_forward(l, gain, shift=None, scale=None, ada=None):
                norm(gain, shift)
                for half, n in (("a", F1), ("b", F2)):
                    seg = SEGS[f"gu{l}{half}"]
                    g0, s0, with_ada = g_count[0], sgs[0], half == "a" and ada is not None

                    def body(i):
                        for k in range(2):
                            f = 2 * i + k
                            t = seg.tile0 + NB * i + 2 * k
                            dve.wait_ge(sg_s, s0 + f + 1)
                            dve.wait_ge(tile_s, t + 2)
                            dve.wait_ge(g_s, g0 + f)
                            nc.vector.tensor_tensor(HF[:, :], SG[:, k, :], PS[:, 2 * k + 1, :], ALU.mult)\
                                .then_inc(evac_s, 2)
                            dve.wait_ge(evac_s, t + 2)
                            split(row(Gh, f), row(Gl, f), HF[:, :], g_s)
                            if with_ada:
                                modulation_unit(ada + f, f, k)
                    loop(dve, 0, n // 2, [(chain, 2 + (14 if with_ada else 0))], body)
                    g_count[0] += n
                    sgs[0] += n
                    if with_ada:
                        dve.wait_ge(mod_sum, l + 1)
                        nc.vector.tensor_tensor(MOD[:, 24 * l:24 * l + 24], PS[:, 5, 0:24],
                                                pcol("bada", 24 * l, 24), ALU.add).then_inc(mod_done, 1)
                    residual(f"dn{l}{half}", scale, squares=half == "b" and l < 2)

            def modulation_unit(n, f, slot):
                dve.wait_ge(ada_s[slot], 8 * n - 8 * slot + 16)
                acc = AACC[:, DS(256 * f, 256)]
                for c in range(DC):
                    w = AW[:, slot, c * 256:c * 256 + 256]
                    if c == 0:
                        chain.mark(nc.vector.tensor_scalar(acc, w, CSIL[:, 0:1], None, ALU.mult))
                        chain.wait()
                    elif c < DC - 1:
                        chain.mark(nc.vector.scalar_tensor_tensor(acc, w, CSIL[:, c:c + 1], acc, ALU.mult, ALU.add))
                        chain.wait()
                    else:
                        nc.vector.scalar_tensor_tensor(acc, w, CSIL[:, c:c + 1], acc, ALU.mult, ALU.add)\
                            .then_inc(ada_acc_s, 1)

            nc.vector.memset(EPSC[:, 0:1], EPS1).then_inc(eps_s, 1)
            nc.vector.memset(EPSC[:, 1:2], EPS2).then_inc(eps_s, 1)
            chain.mark(nc.vector.memset(CV[:, 0:2], 0.0))
            chain.wait()
            dve.wait_ge(par_s, 16)
            for m in range(1, DC):
                add_squares(m)
            norm(lambda m: pcol("a_norm", m))
            conv_mixer()
            residual("wout")
            dve.wait_ge(cs_s, 1)
            feed_forward(0, lambda m: pcol("f_norm0", m), ada=0)
            def split_padded(wh, wl, w, n, done):
                src = w.rearrange("p (c m) -> p c m", c=DC)
                for t in (wh, wl):
                    chain.mark(nc.vector.memset(t[:, :, n:P].bitcast(F32), 0.0))
                chain.mark(nc.vector.tensor_copy(wh[:, :, 0:n], src))
                chain.wait()
                nc.vector.tensor_tensor(wl[:, :, 0:n], src, wh[:, :, 0:n].bitcast(F32), ALU.subtract)\
                    .then_inc(done, 1)

            def copy_tiles(name, dst, turns, scale=None, first=0):
                seg = SEGS[name]

                def body(i):
                    for b in range(NB):
                        n = NB * i + b
                        dve.wait_ge(tile_s, seg.tile0 + n + 1)
                        if scale is None:
                            nc.vector.tensor_copy(dst(n), PS[:, b, :]).then_inc(evac_s, 1)
                        else:
                            nc.vector.tensor_scalar(dst(n), PS[:, b, :], scale, None, ALU.mult).then_inc(evac_s, 1)
                loop(dve, first, turns, [], body)

            def compress_rows():
                dve.wait_ge(h_s, h_count[0])
                chain.mark(nc.vector.memset(XJ[:, :, :, :, :], 0.0))
                chain.mark(nc.vector.memset(KC[:, :, :, :], 0.0))
                chain.wait()
                for s in range(2):
                    dve.wait_ge(rw_s[s], 128)
                    for j in range(16):
                        ins = nc.vector.tensor_scalar(XJ[:, s, j, :, 0:NCMP],
                                                      RW[s][:, :, 2 * j:2 * j + 16 * (NCMP - 1) + 1:16],
                                                      pcol("pek" if s == 0 else "pev", j), None, ALU.add)
                        if j % 4 == 3:
                            ins.then_inc(xj_s, 1)

            def compressed_attention():
                dve.wait_ge(dist_s, 32)
                dve.wait_ge(gt_s, 1)

                def heads(x):
                    return x.rearrange("p (h n) -> p h n", n=CG)

                def wide(x):
                    return x.unsqueeze(2).to_broadcast([P, NH, CG])

                def scores(qb):
                    sc = SC[:, qb % 2, :]
                    if qb:
                        dve.wait_ge(sc_m, qb)
                    chain.mark(nc.vector.tensor_tensor(
                        heads(CB[:, :]), DISTC[:, qb, :].unsqueeze(1).to_broadcast([P, NH, CG]),
                        wide(slopes[:, 0:NH]), ALU.mult))
                    chain.wait()
                    dve.wait_ge(sc_t, qb + 1)
                    if qb >= 2:
                        dve.wait_ge(sc_e, qb - 1)
                    chain.mark(nc.vector.tensor_tensor(sc, CB[:, :], PS[:, 4 + qb % 2, :], ALU.add))
                    chain.wait()
                    chain.mark(nc.vector.tensor_reduce(CMX[:, 0, :], heads(sc), AX_X, ALU.max))
                    chain.wait()
                    nc.vector.tensor_tensor(heads(sc), heads(sc), wide(CMX[:, 0, :]), ALU.subtract)\
                        .then_inc(sc_m, 1)

                def normalize(qb):
                    se = SE[:, qb % 2, :]
                    dve.wait_ge(sc_e, qb + 1)
                    if qb:
                        dve.wait_ge(sc_n, qb)
                    chain.mark(nc.vector.tensor_reduce(CMX[:, 1, :], heads(se), AX_X, ALU.add))
                    chain.wait()
                    chain.mark(nc.vector.reciprocal(CMX[:, 2, :], CMX[:, 1, :]))
                    chain.wait()
                    gate = GT[:, qb, 0:3 * NH:3]
                    if qb == 0:
                        chain.mark(nc.vector.scalar_tensor_tensor(CMX[:, 1, :], CMX[:, 2, :], visrow, gate,
                                                                  ALU.mult, ALU.mult))
                    else:
                        chain.mark(nc.vector.tensor_tensor(CMX[:, 1, :], CMX[:, 2, :], gate, ALU.mult))
                    chain.wait()
                    nc.vector.tensor_tensor(heads(se), heads(se), wide(CMX[:, 1, :]), ALU.mult)\
                        .then_inc(sc_n, 1)
                for qb in range(QB + 1):
                    if qb < QB:
                        scores(qb)
                    if qb:
                        normalize(qb - 1)

            def attention():
                def turn(first, i, base):
                    def shift(k):
                        pp, hf, qb = k // 16, k // 8 % 2, k % 4
                        w = P * qb + P
                        dve.wait_ge(s_t, base(32) + k + 1)
                        dve.wait_ge(bias_s, base(4) + 2 * pp + hf + 1)
                        if k >= 6 or not first:
                            dve.wait_ge(p_t, base(32) + max(k - 5, 0))
                        if not isinstance(i, int):
                            dve.sem_inc(v_step, 1)
                        chain.mark(nc.vector.tensor_tensor_reduce(
                            out=PB[:, k % 6, 0:w], in0=PS[:, (4, 5, 6, 2)[k % 4], 0:w], in1=BIAS[:, 2 * pp + hf, T - w:T],
                            scale=1.0, scalar=-3.0e38, op0=ALU.add, op1=ALU.max, accum_out=NMX[:, 0, k:k + 1]))
                        chain.wait()
                        nc.vector.tensor_scalar(NMX[:, 1, k:k + 1], NMX[:, 0, k:k + 1], -1.0, None, ALU.mult)\
                            .then_inc(s_m, 1)

                    def scale(k):
                        pp, hf, br, qb = k // 16, k // 8 % 2, k // 4 % 2, k % 4
                        w = P * qb + P
                        dve.wait_ge(s_e, base(32) + k + 1)
                        chain.mark(nc.vector.reciprocal(SMX[:, 1, k:k + 1], SMX[:, 0, k:k + 1]))
                        chain.wait()
                        h = 8 * kt + 4 * hf + 2 * (i - 2 * kt) + pp
                        gate = GT[:, qb, DS(3 * h + 1 + br, 1)]
                        nc.vector.tensor_scalar(PB[:, k % 6, 0:w], PB[:, k % 6, 0:w], SMX[:, 1, k:k + 1], gate,
                                                ALU.mult, ALU.mult).then_inc(s_n, 1)

                    def out_pair(pp):
                        pair = 2 * i + pp
                        dve.wait_ge(o_t, base(8) + 4 * pp + 4)
                        chain.mark(nc.vector.tensor_tensor(XO[:, :], row(OC, pair), PS[:, pp, :], ALU.add))
                        chain.wait()
                        split(row(Hh, pair), row(Hl, pair), XO[:, :], o_s)
                        dve.wait_ge(o_s, base(2) + pp + 1)

                    for k in range(32 + 2):
                        if k < 32:
                            shift(k)
                        if k >= 2:
                            scale(k - 2)
                        if k == 25:
                            out_pair(0)
                    out_pair(1)

                per = 32 + 32 + 2 * 2
                for kt in range(2):
                    if kt == 0:
                        turn(True, 0, lambda k: 0)
                        loop(dve, 1, 2, [(chain, per)], lambda i: turn(False, i, lambda k: k * i))
                    else:
                        loop(dve, 2, 4, [(chain, per)], lambda i: turn(False, i, lambda k: k * i))

            kv_end = SEGS["wkv"].tile0 + 12
            norm(lambda m: pcol("kv_norm", m))
            copy_tiles("wkv", lambda n: row(KV, n), 3)
            norm(lambda m: pcol("b_norm", m), again=kv_end)
            dve.wait_ge(vt_s, 4)
            compress_rows()
            copy_tiles("wq", lambda n: row(QT, n), 1, HD ** -0.5)
            dve.wait_ge(xj_used, 4)
            split_padded(GWH, GWL, pcol("gatew", 0, 3 * NH * DC), 3 * NH, gw_s)
            copy_tiles("wq", lambda n: row(QT, n), 2, HD ** -0.5, first=1)
            compressed_attention()
            attention()
            residual("wo")
            feed_forward(1, lambda m: pcol("f_norm1", m), ada=12)
            def stick_breaking(r):
                seg = SEGS["qkv"]

                def normalize(n):
                    dve.wait_ge(r2_s, 8 * r + n + 1)
                    nc.vector.scalar_tensor_tensor(QKV[:, n, :], QKV[:, n, :], pcol("qn" if n < 4 else "kn"),
                                                   RT2[:, n % 2, :], ALU.mult, ALU.mult).then_inc(qk_s, 1)
                for n in range(12):
                    dve.wait_ge(tile_s, seg.tile0 + 12 * r + n + 1)
                    nc.vector.tensor_copy(QKV[:, n, :], PS[:, n % NB, :]).then_inc(evac_s, 1)
                    if 2 <= n < 10:
                        normalize(n - 2)

                def logits(k):
                    w = P * (k % 4) + P
                    dve.wait_ge(ss_t, 32 * r + k + 1)
                    if k >= 3:
                        dve.wait_ge(ss_w, 32 * r + k - 2)
                    chain.mark(nc.vector.scalar_tensor_tensor(XM[:, k % 3, 0:w], PS[:, 4 + k % 4, 0:w], HD ** -0.5,
                                                              MW[:, T - w:T], ALU.mult, ALU.add))
                    chain.wait()
                    nc.vector.scalar_tensor_tensor(EE[:, k % 2, 0:w], XM[:, k % 3, 0:w], -1.0,
                                                   XM[:, k % 3, 0:w], ALU.mult, ALU.min).then_inc(ss_x, 1)

                def sums(k):
                    w = P * (k % 4) + P
                    dve.wait_ge(ss_l, 32 * r + k + 1)
                    chain.mark(nc.vector.scalar_tensor_tensor(EE[:, k % 2, 0:w], XM[:, k % 3, 0:w], 0.0,
                                                              EE[:, k % 2, 0:w], ALU.max, ALU.add))
                    chain.wait()
                    if k >= 6:
                        dve.wait_ge(st_t, 32 * r + k - 5)
                    nc.vector.tensor_tensor_scan(CC[:, k % 6, 0:w][:, ::-1], ones[:, 0:1].to_broadcast([P, w]),
                                                 EE[:, k % 2, 0:w][:, ::-1], 0.0, ALU.mult, ALU.add)\
                        .then_inc(ss_c, 1)

                def out_pair(a):
                    dve.wait_ge(so_t, 8 * r + 2 * a + 2)
                    split(row(Gh, 4 * r + a), row(Gl, 4 * r + a), PS[:, 2 + a % 2, :], so_s)
                for k in range(33):
                    if k < 32:
                        logits(k)
                    if k:
                        sums(k - 1)
                    if k % 8 == 0 and k > 8:
                        out_pair(k // 8 - 2)
                out_pair(3)

            def conv_xbc():
                seg = SEGS["xbc"]

                def body(i):
                    for b in range(NB):
                        t = NB * i + b
                        dve.wait_ge(tile_s, seg.tile0 + t + 1)
                        nc.vector.tensor_copy(RB[:, 3:T + 3], PS[:, b, :]).then_inc(evac_s, 1)
                        dve.wait_ge(evac_s, seg.tile0 + t + 1)
                        if not isinstance(i, int) or t >= 2:
                            dve.wait_ge(xb_s, t - 1)
                        acc = CA[:, b % 2, :]
                        chain.mark(nc.vector.tensor_scalar(acc, RB[:, 0:T], pcol("conv2", t),
                                                           pcol("conv2b", t), ALU.mult, ALU.add))
                        chain.wait()
                        for tap in range(1, 4):
                            ins = nc.vector.scalar_tensor_tensor(acc, RB[:, tap:T + tap], pcol("conv2", 12 * tap + t),
                                                                 acc, ALU.mult, ALU.add)
                            if tap < 3:
                                chain.mark(ins)
                                chain.wait()
                            else:
                                ins.then_inc(ca_s, 1)
                                dve.wait_ge(ca_s, t + 1)
                body(0)
                dt_rows()
                loop(dve, 1, 3, [(chain, 12)], body)

            def dt_rows():
                dve.wait_ge(dt_t, 1)
                flat = "p q h -> p (q h)"
                bias = pcol("dtb", 0, NH).unsqueeze(1).to_broadcast([P, QB, NH])
                nc.vector.tensor_tensor(DT[:, :, :], PS[:, 7, 0:QB * NH].rearrange("p (q h) -> p q h", q=QB), bias,
                                        ALU.add).then_inc(dt_a, 1)
                dve.wait_ge(dt_a, 1)
                nc.vector.scalar_tensor_tensor(DTE[:, :, :].rearrange(flat), DT[:, :, :].rearrange(flat), -1.0,
                                               DT[:, :, :].rearrange(flat), ALU.mult, ALU.min).then_inc(dt_a, 1)
                dve.wait_ge(dt_e, 2)
                chain.mark(nc.vector.scalar_tensor_tensor(DT[:, :, :].rearrange(flat), DT[:, :, :].rearrange(flat), 0.0,
                                                          DTE[:, :, :].rearrange(flat), ALU.max, ALU.add))
                chain.wait()
                nc.vector.scalar_tensor_tensor(ADT[:, :, :], DT[:, :, :], -1.0,
                                               AN[:, :].unsqueeze(1).to_broadcast([P, QB, NH]), ALU.mult,
                                               ALU.mult).then_inc(dt_s, 1)

            def cumulative_sums():
                flat = "p q h -> p (q h)"
                dve.wait_ge(cs_t, 1)
                chain.mark(nc.vector.tensor_copy(CS[:, :, :].rearrange(flat), PS[:, 6, 0:QB * NH]))
                chain.mark(nc.vector.memset(PREV[:, :, :], 0.0))
                chain.wait()
                nc.vector.tensor_scalar(NCS[:, :, :].rearrange(flat), CS[:, :, :].rearrange(flat), -1.0, None,
                                        ALU.mult).then_inc(ncs_s, 1)

            def attention_part(m):
                dve.wait_ge(tile_s, SEGS["wog"].tile0 + m + 1)
                nc.vector.scalar_tensor_tensor(X[:, m, :], PS[:, 7, :], MOD[:, 16 + m:17 + m], X[:, m, :], ALU.mult,
                                               ALU.add).then_inc(evac_s, 1)

            def ssd_chunk(c):
                def small(x):
                    return x[:, DS(c, 1), :].rearrange("p a h -> p (a h)")

                def per_head(x):
                    return x.unsqueeze(2).to_broadcast([P, NH, HD])

                def bank_rows(b):
                    return PS[:, b:b + 2, :].rearrange("p b (h d) -> p (b h) d", d=HD)
                nc.vector.tensor_copy(ADTC[:, :], small(ADT)).then_inc(ac_s, 1)
                dve.wait_ge(xt_t, c + 1)
                chain.mark(nc.vector.tensor_tensor(XDT[:, :, :], bank_rows(2), per_head(small(DT)), ALU.mult))
                chain.mark(nc.vector.tensor_copy(SCR[:, :, :].rearrange("p g l -> p (g l)"), PS[:, 4, 0:2 * P]))
                chain.mark(nc.vector.tensor_copy(BTK[:, :, :].rearrange("p g l -> p (g l)"), PS[:, 4, 2 * P:4 * P]))
                for q in range(2):
                    dve.wait_ge(cb_t, 2 * c + q + 1)
                    chain.mark(nc.vector.tensor_copy(CSL[:, 8 * q:8 * q + 8].rearrange("p (b h) -> p b h", b=2),
                                                     PS[:, 0:2, P - 1:4 * P:P]))
                    nc.vector.tensor_tensor(LM[:, 8 * q:8 * q + 8, :],
                                            PS[:, 0:2, :].rearrange("p b (h l) -> p (b h) l", l=P),
                                            MASKL.unsqueeze(1).to_broadcast([P, 8, P]), ALU.add).then_inc(lm_s, 1)
                chain.wait()
                chain.mark(nc.vector.tensor_tensor(EX[:, 0, :], CSL[:, :], small(CS), ALU.subtract))
                chain.mark(nc.vector.tensor_copy(EX[:, 1, :], CSL[:, :]))
                nc.vector.tensor_copy(EX[:, 2, :], small(CS)).then_inc(ex_s, 1)
                for q in range(2):
                    dve.wait_ge(le_s, 2 * c + q + 1)
                    nc.vector.tensor_tensor(LM[:, 8 * q:8 * q + 8, :], LM[:, 8 * q:8 * q + 8, :],
                                            SCR[:, q, :].unsqueeze(1).to_broadcast([P, 8, P]), ALU.mult)\
                        .then_inc(mm_s, 1)
                dve.wait_ge(de_s, c + 1)
                nc.vector.tensor_tensor(XDD[:, :, :], XDT[:, :, :], per_head(EX[:, 0, :]), ALU.mult)\
                    .then_inc(xdt_s, 1)
                attention_part(2 * c)
                dve.wait_ge(yd_t, c + 1)
                chain.mark(nc.vector.tensor_tensor(YC[:, :, :], bank_rows(5), per_head(EX[:, 2, :]), ALU.mult))
                chain.mark(nc.vector.tensor_tensor(PREV[:, :, :], PREV[:, :, :], per_head(EX[:, 1, :]), ALU.mult))
                chain.wait()
                nc.vector.tensor_tensor(YC[:, :, :], YC[:, :, :], bank_rows(2), ALU.add).then_inc(y_s, 1)
                chain.mark(nc.vector.tensor_tensor(PREV[:, :, :], PREV[:, :, :], bank_rows(0), ALU.add))
                chain.wait()
                attention_part(2 * c + 1)
                dve.wait_ge(yt_t, c + 1)
                for f in range(DC):
                    xs = XB[:, f, DS(P * c, P)]
                    ins = nc.vector.scalar_tensor_tensor(xs, xs, pcol("dskip", f),
                                                         PS[:, 5 + f // 4, (f % 4) * P:(f % 4) * P + P],
                                                         ALU.mult, ALU.add)
                ins.then_inc(ck_s, 1)
                dve.wait_ge(ck_s, c + 1)

            def gated_rows():
                seg = SEGS["zg"]
                for m in range(DC):
                    dve.wait_ge(sz_s, m + 1)
                    nc.vector.tensor_tensor(XB[:, m, :], XB[:, m, :], SZ[:, m % 2, :], ALU.mult).then_inc(evac_s, 1)
                dve.wait_ge(tile_s, seg.tile0 + DC)
                for g in range(2):
                    dve.wait_ge(rz_s, g + 1)
                    for m in range(4 * g, 4 * g + 4):
                        if m >= 2:
                            dve.wait_ge(yo_s, m - 1)
                        chain.mark(nc.vector.scalar_tensor_tensor(XN2[:, m % 2, :], XB[:, m, :], pcol("ssdn", m),
                                                                  RZ[:, g, :], ALU.mult, ALU.mult))
                        chain.wait()
                        split(Hh[:, m, :], Hl[:, m, :], XN2[:, m % 2, :], yo_s)

            def gain_of(weight, scale):
                chain.mark(nc.vector.scalar_tensor_tensor(GM[:, :], MOD[:, scale:scale + DC], 1.0, pcol(weight, 0, DC),
                                                          ALU.add, ALU.mult))
                chain.wait()

            norm(lambda m: pcol("final", m), to_x=xf_s)
            dve.wait_ge(mod_done, 2)
            dve.wait_ge(xf_s, DC)
            gain_of("norm1", 8)
            norm(lambda m: GM[:, DS(m, 1)], shift=lambda m: MOD[:, DS(m, 1)])
            dve.wait_ge(mask_s, 16)
            chain.mark(nc.vector.memset(MW[:, 0:T - P], 0.0))
            chain.mark(nc.vector.tensor_copy(MW[:, T - P:T], MASK))
            chain.wait()
            loop(dve, 0, 2, [(chain, 32 + 32 + 4)], stick_breaking)
            dve.wait_ge(so_s, DC)
            split_padded(DWH, DWL, pcol("dtw", 0, DC * NH), NH, dw_s)
            chain.mark(nc.vector.memset(RB[:, 0:3], 0.0))
            chain.wait()
            conv_xbc()
            cumulative_sums()
            for c in range(QB):
                ssd_chunk(c)
            gated_rows()
            residual("woh", lambda m: MOD[:, DS(16 + m, 1)])
            gain_of("norm2", 32)
            feed_forward(2, lambda m: GM[:, DS(m, 1)], shift=lambda m: MOD[:, DS(24 + m, 1)],
                         scale=lambda m: MOD[:, DS(40 + m, 1)])





def kernel(**inputs):
    import numpy as np
    import concourse.bacc as bacc
    from concourse.bass_utils import run_bass_kernel_spmd as run

    a = {k: np.asarray(v) for k, v in inputs.items()}

    def tiles(w, chunks=None):
        k, m = w.shape
        return w.reshape(k // P, P, m // P, P).transpose(2, 1, 0, 3)

    def units(t, n):
        u = t.reshape(t.shape[0] // n, n, *t.shape[1:])
        return u.transpose(0, 2, 3, 1, 4).reshape(u.shape[0], P, -1)

    w_in = tiles(a["a_w_in"][0]).reshape(3, DC, P, DC, P)
    w_in = w_in[[1, 2, 0]].transpose(1, 0, 2, 3, 4).reshape(3 * DC, P, DC, P)
    kinds = {k: [] for k in KINDS}

    def ff(gate, up, down):
        g, u = tiles(gate), tiles(up)
        pair = np.stack([g, u], 1).reshape(2 * FC, P, DC, P)
        dn = tiles(down)
        kinds["A"].append(units(pair, 2))
        kinds["B"].append(units(dn[:, :, 0:F1], 1))
        kinds["C"].append(units(dn[:, :, F1:FC], 1))

    f_gu, f_dn = a["f_w_gu"], a["f_w_down"]
    kinds["A"] += [units(w_in, 2), units(tiles(a["a_w_out"][0]), 2)]
    ff(f_gu[0][:, :F], f_gu[0][:, F:], f_dn[0])
    kinds["A"].append(units(tiles(a["w_kv"]), 2))
    order = [8 * p + j + 4 * h for p in range(2) for j in range(4) for h in range(2)]
    qg = a["b_w_qg"][0]
    wq = qg[:, :NH * HD].reshape(D, NH, HD)[:, order].reshape(D, NH * HD)
    kinds["A"].append(units(tiles(wq), 2))
    wo = a["b_w_o"][0].reshape(NH, HD, D)[order].reshape(NH * HD, D)
    kinds["A"].append(units(tiles(wo), 2))
    ff(f_gu[1][:, :F], f_gu[1][:, F:], f_dn[1])
    wi = a["w_in_2"][0]
    z, xbc, dtw, q, k, v = (wi[:, lo:hi] for lo, hi in
                            ((0, 1024), (1024, 2560), (2560, 2576), (2576, 3600), (3600, 4624), (4624, 5648)))
    q, k, v = tiles(q), tiles(k), tiles(v)
    for r in range(2):
        kinds["A"].append(units(np.concatenate([w[4 * r:4 * r + 4] for w in (q, k, v)]), 2))
    w_out = a["w_out_2"][0]
    kinds["A"] += [units(tiles(w), 2) for w in (xbc, w_out[D:], z, w_out[:D])]
    ff(a["w_gate_2"][0], a["w_up_2"][0], a["w_down_2"][0])

    def cols(w):
        return w.reshape(-1, P).T

    def rows(w, n):
        return w.reshape(n, P, -1).transpose(1, 0, 2).reshape(P, -1)

    def wide(w):
        return np.broadcast_to(w[None, :], (P, w.shape[0]))

    w2k = rows(np.concatenate([a["cmp_w2_k"]] * 2, 1), 2)
    par = {
        "a_norm": cols(a["a_norm"][0]), "f_norm0": cols(a["f_norm"][0]), "kv_norm": cols(a["kv_norm"]),
        "b_norm": cols(a["b_norm"][0]), "f_norm1": cols(a["f_norm"][1]), "final": cols(a["final_norm"]),
        "norm1": cols(a["norm1_w_2"][0]), "norm2": cols(a["norm2_w_2"][0]),
        "conv1": cols(a["a_conv"][0].reshape(-1)), "conv2": cols(a["conv_w_2"][0].reshape(-1)),
        "conv2b": cols(a["conv_b_2"][0]), "ssdn": cols(a["ssd_norm_w_2"][0]),
        "dskip": cols(np.broadcast_to(a["d_skip_2"][0][:, None], (NH, HD)).reshape(-1)),
        "qn": cols(np.concatenate([a["q_norm_w_2"][0]] * 2)), "kn": cols(np.concatenate([a["k_norm_w_2"][0]] * 2)),
        "bada": cols(a["b_ada_2"][0]), "cond": cols(a["c_2"][0]),
        "pek": cols(a["cmp_pe_k"].reshape(-1)), "pev": cols(a["cmp_pe_v"].reshape(-1)),
        "dtb": wide(a["dt_bias_2"][0]), "alog": wide(a["a_log_2"][0]),
        "gatew": rows(qg[:, NH * HD:], DC), "dtw": rows(dtw, DC), "w2k": w2k, "w2v": rows(a["cmp_w2_v"], 2),
    }
    for n, w in PARAMS:
        assert par[n].shape == (P, w), (n, par[n].shape, w)
    arrays = {
        "x_in": a["x"][0].reshape(T, DC, P).transpose(2, 1, 0),
        **{f"w{k}": np.concatenate(v) for k, v in kinds.items()},
        "wada": units(tiles(a["w_ada_2"][0]), 2),
        "w1k": rows(a["cmp_w1_k"], 16), "w1v": rows(a["cmp_w1_v"], 16),
        "par": np.concatenate([par[n] for n, _ in PARAMS], 1),
    }
    p, y = np.arange(P)[:, None], np.arange(T)[None, :]
    dist = np.where(y > p + T - P, BIG, p + T - P - y)
    qb, n = np.arange(QB)[None, :, None], np.arange(CG)[None, None, :]
    tok = p[:, :, None] + P * qb
    distc = np.where(16 * n + 31 > tok, BIG, tok - 16 * n - 15.5).reshape(P, -1)
    c = np.zeros((P, C_END), np.float32)
    c[:, C_IDENT:C_IDENT + P] = p == y[:, :P]
    c[:, C_BONES:C_BONES + P] = p // HD == y[:, :P] // HD
    c[:, C_SLOPES:C_SLOPES + NH] = -np.exp2(-8.0 * np.arange(1, NH + 1) / NH)[None, :]
    c[:, C_VIS:C_VIS + 1] = p >= 31
    c[:, C_DIST:C_DIST + T] = dist
    c[:, C_DISTC:C_DISTC + QB * CG] = distc
    c[:, C_TRI:C_TRI + P] = p <= y[:, :P]
    c[:, C_MASKL:C_MASKL + P] = np.where(p <= y[:, :P], 0.0, -BIG)
    c[:, C_MASK:C_MASK + P] = np.where(y[:, :P] < p, 0.0, -BIG)
    arrays["consts"] = c
    nc = bacc.Bacc("TRN2", target_bir_lowering=False, num_devices=1)
    arrays = {k: np.ascontiguousarray(v) for k, v in arrays.items()}
    args = [nc.dram_tensor(k, v.shape, F32, kind="ExternalInput").ap() for k, v in arrays.items()]
    out = nc.dram_tensor("out", (P, DC, T), F32, kind="ExternalOutput").ap()
    two_blocks(nc, *args, out)
    got = run(nc, [arrays], core_ids=[0]).results[0]["out"]
    return np.ascontiguousarray(got.transpose(2, 1, 0).reshape(1, T, D))
```
